# Optimizing a Trainium2 kernel written in Bass

```python
import math
import jax, jax.numpy as jnp
from jax import lax
import numpy as np

D_MODEL = 1024
BATCH = 1
SEQ = 256
DEPTH = 1

HEAD_DIM = 64
N_FOX_HEADS = D_MODEL // 128
N_DIFF_HEADS = D_MODEL // 256
DIFF_V_DIM = 2 * HEAD_DIM
FOX_WIDTH = N_FOX_HEADS * HEAD_DIM
DIFF_QK_WIDTH = N_DIFF_HEADS * 2 * HEAD_DIM
DIFF_WIDTH = N_DIFF_HEADS * DIFF_V_DIM
MIX_WIDTH = FOX_WIDTH + DIFF_WIDTH
FOX_Q0 = 0
FOX_K0 = FOX_Q0 + FOX_WIDTH
FOX_V0 = FOX_K0 + FOX_WIDTH
FOX_F0 = FOX_V0 + FOX_WIDTH
DIFF_Q0 = FOX_F0 + N_FOX_HEADS
DIFF_K0 = DIFF_Q0 + DIFF_QK_WIDTH
DIFF_V0 = DIFF_K0 + DIFF_QK_WIDTH
IN_WIDTH = DIFF_V0 + DIFF_WIDTH

BLOCK_Q = 128
NUM_BUCKETS = 32
MAX_DISTANCE = 128
N_EXPERTS = 32
TOP_K = 4
D_FF = D_MODEL
SWIGLU_ALPHA = 1.702
SWIGLU_LIMIT = 7.0
MOE_BLOCK = 256
PLE_DIM = 256
NORM_EPS = 1e-6
NEG_INF = -1e30

kernel_name = 'hybrid_fox_diffattn_moe_ple'

def rms_norm(x, g):
    xf = x.astype(jnp.float32)
    y = xf * lax.rsqrt(jnp.mean(xf * xf, axis=-1, keepdims=True) + NORM_EPS)
    return (y * g.astype(jnp.float32)).astype(x.dtype)

def causal_mask(q0, q1):
    qpos = jnp.arange(q0, q1, dtype=jnp.int32)
    kpos = jnp.arange(q1, dtype=jnp.int32)
    return kpos[None, :] <= qpos[:, None], qpos[:, None] - kpos[None, :]

def t5_bucket(rel):
    n = jnp.maximum(rel, 0)
    max_exact = NUM_BUCKETS // 2
    nf = jnp.maximum(n, 1).astype(jnp.float32)
    large = max_exact + (jnp.log(nf / max_exact) / math.log(MAX_DISTANCE / max_exact)
                         * (NUM_BUCKETS - max_exact)).astype(jnp.int32)
    large = jnp.minimum(large, NUM_BUCKETS - 1)
    return jnp.where(n < max_exact, n, large)

def fox_attention(q, k, v, logf):
    seq = q.shape[2]
    scale = HEAD_DIM ** -0.5
    c = jnp.cumsum(logf, axis=-1)
    outs = []
    for blk in range(seq // BLOCK_Q):
        q0, q1 = blk * BLOCK_Q, (blk + 1) * BLOCK_Q
        mask, _ = causal_mask(q0, q1)
        s = jnp.einsum('bhqd,bhkd->bhqk', q[:, :, q0:q1], k[:, :, :q1]).astype(jnp.float32) * scale
        s = s + c[:, :, q0:q1, None] - c[:, :, None, :q1]
        s = jnp.where(mask, s, NEG_INF)
        pr = jax.nn.softmax(s, axis=-1).astype(v.dtype)
        outs.append(jnp.einsum('bhqk,bhkd->bhqd', pr, v[:, :, :q1]))
    return jnp.concatenate(outs, axis=2)

def diff_attention(q1, q2, k1, k2, v, rel_table, lam):
    seq = q1.shape[2]
    scale = HEAD_DIM ** -0.5
    outs = []
    for blk in range(seq // BLOCK_Q):
        q0, qe = blk * BLOCK_Q, (blk + 1) * BLOCK_Q
        mask, rel = causal_mask(q0, qe)
        bias = jnp.take(rel_table, t5_bucket(rel), axis=0).astype(jnp.float32)
        bias = jnp.transpose(bias, (2, 0, 1))[None]
        s1 = jnp.einsum('bhqd,bhkd->bhqk', q1[:, :, q0:qe], k1[:, :, :qe]).astype(jnp.float32) * scale + bias
        s2 = jnp.einsum('bhqd,bhkd->bhqk', q2[:, :, q0:qe], k2[:, :, :qe]).astype(jnp.float32) * scale + bias
        a1 = jax.nn.softmax(jnp.where(mask, s1, NEG_INF), axis=-1)
        a2 = jax.nn.softmax(jnp.where(mask, s2, NEG_INF), axis=-1)
        pr = (a1 - lam * a2).astype(v.dtype)
        outs.append(jnp.einsum('bhqk,bhkd->bhqd', pr, v[:, :, :qe]))
    return jnp.concatenate(outs, axis=2)

def clamped_swiglu(h):
    x_glu = jnp.minimum(h[..., ::2], SWIGLU_LIMIT)
    x_lin = jnp.clip(h[..., 1::2], -SWIGLU_LIMIT, SWIGLU_LIMIT)
    return x_glu * jax.nn.sigmoid(SWIGLU_ALPHA * x_glu) * (x_lin + 1.0)

def moe(xm, w_router, b_router, w1, b1, w2, b2):
    bsz, seq, d = xm.shape
    n_tok = bsz * seq
    xs = xm.reshape(n_tok, d)
    logits = (xs @ w_router + b_router).astype(jnp.float32)
    top_v, top_i = lax.top_k(logits, TOP_K)
    gates = jax.nn.softmax(top_v, axis=-1)
    m = n_tok * TOP_K
    e_flat = top_i.reshape(m)
    g_flat = gates.reshape(m)
    tok_flat = jnp.broadcast_to(jnp.arange(n_tok, dtype=jnp.int32)[:, None], (n_tok, TOP_K)).reshape(m)
    order = jnp.argsort(e_flat, stable=True)
    e_sorted = e_flat[order]
    counts = jnp.bincount(e_flat, length=N_EXPERTS)
    starts = jnp.cumsum(counts) - counts
    padded = ((counts + MOE_BLOCK - 1) // MOE_BLOCK) * MOE_BLOCK
    pad_ends = jnp.cumsum(padded)
    pad_starts = pad_ends - padded
    dest = pad_starts[e_sorted] + (jnp.arange(m, dtype=jnp.int32) - starts[e_sorted])
    n_blocks = (m + N_EXPERTS * MOE_BLOCK + MOE_BLOCK - 1) // MOE_BLOCK
    p_rows = n_blocks * MOE_BLOCK
    buf_tok = jnp.zeros((p_rows,), jnp.int32).at[dest].set(tok_flat[order])
    buf_gate = jnp.zeros((p_rows,), jnp.float32).at[dest].set(g_flat[order])
    block_start = jnp.arange(n_blocks, dtype=jnp.int32) * MOE_BLOCK
    block_expert = jnp.minimum(jnp.searchsorted(pad_ends, block_start, side='right'), N_EXPERTS - 1)

    def block_fn(args):
        tok, e = args
        xb = xs[tok]
        hb = clamped_swiglu(xb @ w1[e] + b1[e])
        return hb @ w2[e] + b2[e]

    outs = lax.map(block_fn, (buf_tok.reshape(n_blocks, MOE_BLOCK), block_expert))
    outs = outs.reshape(p_rows, d) * buf_gate[:, None].astype(outs.dtype)
    y = jnp.zeros((n_tok, d), outs.dtype).at[buf_tok].add(outs)
    return y.reshape(bsz, seq, d).astype(xm.dtype)

def setup_inputs(seed: int = 0) -> dict:
    key = jax.random.key(seed)
    ks = jax.random.split(key, 26)
    f32 = jnp.float32
    nrm = lambda k, shape, s: jax.random.normal(k, shape, f32) * s
    gain = lambda k, shape: 1.0 + 0.02 * jax.random.normal(k, shape, f32)
    return {
        'x': nrm(ks[0], (BATCH, SEQ, D_MODEL), 1.0),
        'p': nrm(ks[1], (DEPTH, BATCH, SEQ, PLE_DIM), 1.0),
        'rel_bias': nrm(ks[2], (NUM_BUCKETS, N_DIFF_HEADS), 0.3),
        'g_attn': gain(ks[3], (DEPTH, D_MODEL)),
        'w_in': nrm(ks[4], (DEPTH, D_MODEL, IN_WIDTH), D_MODEL ** -0.5),
        'b_f': 3.0 + 0.5 * jax.random.normal(ks[5], (DEPTH, N_FOX_HEADS), f32),
        'g_fox_q': gain(ks[6], (DEPTH, HEAD_DIM)),
        'g_fox_k': gain(ks[7], (DEPTH, HEAD_DIM)),
        'g_diff_q': gain(ks[8], (DEPTH, HEAD_DIM)),
        'g_diff_k': gain(ks[9], (DEPTH, HEAD_DIM)),
        'lambda_q1': nrm(ks[10], (DEPTH, HEAD_DIM), 0.1),
        'lambda_k1': nrm(ks[11], (DEPTH, HEAD_DIM), 0.1),
        'lambda_q2': nrm(ks[12], (DEPTH, HEAD_DIM), 0.1),
        'lambda_k2': nrm(ks[13], (DEPTH, HEAD_DIM), 0.1),
        'g_subln': gain(ks[14], (DEPTH, DIFF_V_DIM)),
        'w_out': nrm(ks[15], (DEPTH, MIX_WIDTH, D_MODEL), MIX_WIDTH ** -0.5),
        'g_mlp': gain(ks[16], (DEPTH, D_MODEL)),
        'w_router': nrm(ks[17], (DEPTH, D_MODEL, N_EXPERTS), D_MODEL ** -0.5),
        'b_router': nrm(ks[18], (DEPTH, N_EXPERTS), 0.01),
        'w1': nrm(ks[19], (DEPTH, N_EXPERTS, D_MODEL, 2 * D_FF), D_MODEL ** -0.5),
        'b1': nrm(ks[20], (DEPTH, N_EXPERTS, 2 * D_FF), 0.01),
        'w2': nrm(ks[21], (DEPTH, N_EXPERTS, D_FF, D_MODEL), D_FF ** -0.5),
        'b2': nrm(ks[22], (DEPTH, N_EXPERTS, D_MODEL), 0.01),
        'g_ple': gain(ks[23], (DEPTH, D_MODEL)),
        'w_ple_gate': nrm(ks[24], (DEPTH, D_MODEL, D_MODEL), D_MODEL ** -0.5),
        'w_ple_proj': nrm(ks[25], (DEPTH, PLE_DIM, D_MODEL), PLE_DIM ** -0.5),
    }

def reference(x, p, rel_bias, g_attn, w_in, b_f, g_fox_q, g_fox_k, g_diff_q, g_diff_k,
              lambda_q1, lambda_k1, lambda_q2, lambda_k2, g_subln, w_out, g_mlp,
              w_router, b_router, w1, b1, w2, b2, g_ple, w_ple_gate, w_ple_proj):
    bsz, seq, _ = x.shape
    to_heads = lambda t, nh, hd: t.reshape(bsz, seq, nh, hd).transpose(0, 2, 1, 3)
    h = x
    for i in range(DEPTH):
        a = rms_norm(h, g_attn[i])
        proj = a @ w_in[i]
        fq = rms_norm(to_heads(proj[..., FOX_Q0:FOX_K0], N_FOX_HEADS, HEAD_DIM), g_fox_q[i])
        fk = rms_norm(to_heads(proj[..., FOX_K0:FOX_V0], N_FOX_HEADS, HEAD_DIM), g_fox_k[i])
        fv = to_heads(proj[..., FOX_V0:FOX_F0], N_FOX_HEADS, HEAD_DIM)
        f_logit = (proj[..., FOX_F0:DIFF_Q0] + b_f[i]).astype(jnp.float32)
        logf = jnp.transpose(jax.nn.log_sigmoid(f_logit), (0, 2, 1))
        fox_out = fox_attention(fq, fk, fv, logf)
        fox_out = fox_out.transpose(0, 2, 1, 3).reshape(bsz, seq, FOX_WIDTH)
        dq = proj[..., DIFF_Q0:DIFF_K0].reshape(bsz, seq, N_DIFF_HEADS, 2, HEAD_DIM)
        dk = proj[..., DIFF_K0:DIFF_V0].reshape(bsz, seq, N_DIFF_HEADS, 2, HEAD_DIM)
        dq = rms_norm(dq, g_diff_q[i]).transpose(0, 2, 3, 1, 4)
        dk = rms_norm(dk, g_diff_k[i]).transpose(0, 2, 3, 1, 4)
        dv = to_heads(proj[..., DIFF_V0:IN_WIDTH], N_DIFF_HEADS, DIFF_V_DIM)
        lam_init = 0.8 - 0.6 * math.exp(-0.3 * i)
        lam = (jnp.exp(jnp.sum(lambda_q1[i].astype(jnp.float32) * lambda_k1[i].astype(jnp.float32)))
               - jnp.exp(jnp.sum(lambda_q2[i].astype(jnp.float32) * lambda_k2[i].astype(jnp.float32)))
               + lam_init)
        diff_out = diff_attention(dq[:, :, 0], dq[:, :, 1], dk[:, :, 0], dk[:, :, 1], dv, rel_bias, lam)
        diff_out = rms_norm(diff_out, g_subln[i]) * (1.0 - lam_init)
        diff_out = diff_out.transpose(0, 2, 1, 3).reshape(bsz, seq, DIFF_WIDTH)
        mixed = jnp.concatenate([fox_out, diff_out.astype(fox_out.dtype)], axis=-1)
        h = h + mixed @ w_out[i]
        h = h + moe(rms_norm(h, g_mlp[i]), w_router[i], b_router[i], w1[i], b1[i], w2[i], b2[i])
        gate = jax.nn.sigmoid(rms_norm(h, g_ple[i]) @ w_ple_gate[i])
        h = h + gate * (p[i] @ w_ple_proj[i])
    return h


_drawn_inputs = setup_inputs


def setup_inputs(seed=0):
    import zlib

    import numpy as np

    out = dict(_drawn_inputs(seed))
    spreads = {}
    factors = {'g_fox_q': 5.014,
     'g_fox_k': 5.149,
     'lambda_q1': 6.816,
     'g_subln': 2.746,
     'b1': 8.0,
     'b2': 8.0,
     'g_ple': 200.0,
     'b_router': 2.892}
    for name, (base, spread) in spreads.items():
        noise = np.random.default_rng([zlib.crc32(name.encode()), seed]).standard_normal(out[name].shape)
        drawn = base * np.exp(spread * noise) if base else spread * noise
        out[name] = __import__('jax').numpy.asarray(drawn.astype(out[name].dtype))
    for name, factor in factors.items():
        out[name] = (out[name] * factor).astype(out[name].dtype)
    return out
```

```python
import numpy as np
import concourse.bass as bass
from concourse import mybir
from concourse.alu_op_type import AluOpType as ALU
from contextlib import ExitStack

F32 = mybir.dt.float32
I32 = mybir.dt.int32
U32 = mybir.dt.uint32
ACT = mybir.ActivationFunctionType
X = mybir.AxisListType.X

P = 128
T = 256
TT = T // P
D = 1024
KD = D // P
FOX_HEADS, DIFF_HEADS, HD, DV = 8, 4, 64, 128
AUG = HD + 2
FOX_F0 = 3 * FOX_HEADS * HD
GROUP = 512
GROUP_COL = [0, 512, 1024, FOX_F0 + 8, FOX_F0 + 520, FOX_F0 + 1032]
UNITS = 12
QK_UNITS = [0, 1, 2, 3, 6, 7, 8, 9]
V_UNITS = [4, 5, 10, 11]
EPS = 1e-6
NEG = -1e30
LAM_INIT = 0.8 - 0.6 * 1.0
ALPHA, LIMIT = 1.702, 7.0
BUCKETS, VROW = 32, 384

E = 32
TOPK = 4
SLOTS = 64
MORE = T // SLOTS - 1
EXTRA = T * TOPK // SLOTS
ITEMS = E + EXTRA
COLS = ITEMS + 2
RING = 12
CH = 2048

ORDER = ([("proj", 0), ("cum", 0)]
         + [s for u in range(1, 5) for s in (("proj", u), ("qkT", u - 1))]
         + [("proj", 5), ("sc", 0), ("sc", 1)]
         + [("proj", 6), ("pt", 0), ("pt", 1), ("sc", 2), ("sc", 3)]
         + [("proj", 7), ("qkT", 6), ("pv", 0), ("pv", 1), ("pt", 2), ("pt", 3), ("sc", 4), ("sc", 5)]
         + [("proj", 8), ("qkT", 7), ("pv", 2), ("pv", 3), ("pt", 4), ("pt", 5), ("sc", 6), ("sc", 7)]
         + [("proj", 9), ("qkT", 8), ("pv", 4), ("pv", 5), ("pt", 6), ("pt", 7)]
         + [("proj", 10), ("qkT", 9), ("pv", 6), ("pv", 7), ("sc", 8), ("sc", 9)]
         + [("proj", 11), ("pt", 8), ("sc", 10), ("sc", 11)]
         + [("mix", 0), ("pt", 9), ("sc", 12), ("sc", 13), ("pv", 8), ("pt", 10), ("sc", 14), ("sc", 15), ("pv", 9),
            ("pt", 11), ("pv", 10), ("pv", 11), ("mix", 1)])


def spread(ap, axis, n):
    dims = [list(d) for d in ap.ap]
    dims.insert(axis, [0, n])
    return bass.AP(ap.tensor, ap.offset, dims)


class Turns:

    def __init__(self, eng, sem):
        self.eng, self.sem, self.n, self.base = eng, sem, 0, 0

    def step(self, ins):
        ins.then_inc(self.sem, 1)
        self.n += 1

    def link(self, ins):
        self.step(ins)
        self.eng.wait_ge(self.sem, self.base + self.n)


def build(nc, a, out):
    with ExitStack() as ctx:
        def sb(name, shape, dt=F32):
            return ctx.enter_context(nc.sbuf_tensor(name, shape, dt))

        def sem(name):
            return ctx.enter_context(nc.semaphore(name))

        ring = sb("ring", [P, RING, CH])
        wide = sb("wide", [P, KD, D])
        hres = sb("hres", [P, TT, D])
        xn = sb("xn", [P, TT, D])
        aT = sb("aT", [P, KD, T])
        junk = aT[:, :, :].rearrange("p k t -> p (k t)").rearrange("p (h n) -> p h n", h=TT)
        ident = sb("ident", [P, P])
        upper = sb("upper", [P, P])
        ones = sb("ones", [P, P])
        gcols = sb("gcols", [P, 3 * KD])
        wf = sb("wf", [P, KD, FOX_HEADS])
        wr = sb("wr", [P, KD, E])
        small = sb("small", [P, 224])
        col = [0]

        def cut(*shape):
            n = int(np.prod(shape))
            v = small[:, col[0]:col[0] + n]
            col[0] += n
            return v if len(shape) == 1 else v.rearrange("p (a b) -> p a b", a=shape[0])

        ssq, rstd, mhalf = cut(TT), cut(TT), cut(8)
        gains = cut(6)
        gq66, gk66, gq2, gk2, gsub, one = (gains[:, i:i + 1] for i in range(6))
        bf, z, zn, ze, logf = cut(8), cut(TT, 8), cut(TT, 8), cut(TT, 8), cut(TT, 8)
        cpos, cneg = cut(TT, 8), cut(TT, 8)
        ms, qr = cut(8), cut(8)
        lam, zlow = cut(6), cut(TT, 8)
        nmax, esum, rsum, nl = cut(2, 2), cut(2, 2), cut(2, 2), cut(2)
        dms, dr = cut(2), cut(2)

        arena = sb("arena", [P, 12576])

        def at(off, *shape):
            n = int(np.prod(shape))
            v = arena[:, off:off + n]
            if len(shape) == 2:
                v = v.rearrange("p (a b) -> p a b", a=shape[0])
            if len(shape) == 3:
                v = v.rearrange("p (a b c) -> p a b c", a=shape[0], b=shape[1])
            return v

        qkn = [at(0, 8, AUG), at(528, 8, AUG)]
        qkn_flat = [at(0, GROUP), at(528, GROUP)]
        fqT, fkT = at(1056, 8, T), at(3104, 8, T)
        vrow = at(1056, DIFF_HEADS, VROW)
        bucket = at(2592, VROW)
        relb = at(2976, DIFF_HEADS)
        lamv = at(2984, 4, HD)
        lamp = at(3240, 2, HD)
        grow = at(3368, P)
        dqT, dkT = at(5152, 4, T), at(6176, 4, T)
        fv, dv = at(7200, TT, GROUP), at(8224, TT, GROUP)
        t5 = at(9248, DIFF_HEADS, T)
        fmask = at(10272, T)
        S = [at(10528, VROW), at(10912, VROW)]
        PT = [at(11296, VROW), at(11680, VROW)]
        sq = at(12064, GROUP)

        b1r, b2r = at(1056, 2 * D), at(3104, D)
        wp, pin = at(1056, TT, D), at(3104, TT, 256)
        pT = at(3616, TT, T)
        o = [4128]

        def take(*shape):
            v = at(o[0], *shape)
            o[0] += int(np.prod(shape))
            return v

        xsel = [take(KD, SLOTS), take(KD, SLOTS)]
        hT = [take(KD, SLOTS), take(KD, SLOTS)]
        glu, lin, sig, prod = take(KD, SLOTS), take(KD, SLOTS), take(KD, SLOTS), take(KD, SLOTS)
        outT, outs = take(KD, 2 * SLOTS), take(D)
        Sel, SG, SGT = take(TT, SLOTS), take(TT, 2 * SLOTS), take(T)
        b1i, P1i, Gi = take(2 * KD, COLS), take(TT, COLS), take(TT, COLS)
        iota1, iotae, iota16, iotap = take(SLOTS), take(E), take(EXTRA), take(1)
        lg, mx8, idxf, e4, es = take(TT, E), take(TT, 8), take(TT, 8), take(TT, 4), take(TT)
        M, G, P1 = take(TT, E), take(TT, E), take(TT, E)
        oh, ohg = at(5152, TT, 4, E), at(5408, TT, 4, E)
        P1T, GT = at(0, T), at(256, T)
        cnt, extra, offs, over = at(512, 1), at(513, 1), at(514, MORE), at(518, MORE)
        Er, Eall, Bneg = at(522, MORE, EXTRA), at(570, COLS), at(620, COLS)
        nv0 = at(670, TT)
        brow = at(672, E)
        assert o[0] <= 12576, o[0]
        idx8 = sb("idx8", [P, TT, 8], U32)
        ints = sb("ints", [1, EXTRA + 1], I32)

        B = [ctx.enter_context(nc.psum_tensor(f"bank{i}", [P, 512], F32)) for i in range(8)]
        Y, H, GB, TB = B[0:4], B[4:6], B[6], B[7]
        skew = nc.dram_tensor("skew", (P, DIFF_HEADS * VROW), F32, kind="Internal").ap()

        names = """consts_made mhalf_made gain_ones gain_scaled masked_bucket vec_loaded head_loaded wf_loaded router_loaded
            gcols_T gcols_ready vrow_T vrow_ready skew_stored t5_loaded
            sums_ready mean_ready pow_done xn_ready xT_done xT_ready
            f_done z_ready fe_ready logf_ready cum_done c_ready lam_ready lam_exp
            proj_done sq_ready qk_scaled v_copied qk_ready turned turned_copied
            sc_done sc_masked sc_max exp_done comb_ready pt_done pt_copied pv_done pv_taken dsum_ready
            mixT_done mixT_copied wout_loaded out_done res_ready
            router_pe router_dve router_act tables_ready b_loaded b_used
            chunk_used sel_ready gath_done gath_taken h_done h_taken glu_ready sig_ready hT_ready
            t_done t_taken o_done o_taken_v o_taken_a sgt_done comb_done
            gate_loaded tail_loaded y_taken pT_done pT_ready pp_done gate_done sg_ready gated y_final stored
            dve_turn act_turn pool_turn""".split()
        s = {n: sem(n) for n in names}
        x_loaded = [sem(f"x_loaded{i}") for i in range(TT)]
        win_loaded = [sem(f"win_loaded{i}") for i in range(RING)]
        chunk_loaded = [sem(f"chunk_loaded{i}") for i in range(RING)]

        w_in = a["w_in"][0]
        w1, w2 = a["w1"][0], a["w2"][0]

        def rows(ap):
            return ap.rearrange("(k p) n -> p k n", p=P)

        def unit_free(eng, u):
            if u in QK_UNITS:
                eng.wait_ge(s["qk_scaled"], QK_UNITS.index(u) + 1)
            else:
                eng.wait_ge(s["v_copied"], V_UNITS.index(u) + 1)

        turned_after, n_turned = {}, 0
        for step, i in ORDER:
            n_turned += {"qkT": 2 if i < 4 else 1, "pt": 1, "mix": 2}.get(step, 0)
            turned_after[step, i] = n_turned
        powers_before, n_powers = {}, TT
        for step, i in ORDER:
            if (step == "proj" and i in QK_UNITS) or (step == "pv" and i >= 8):
                powers_before[step, i] = n_powers
                n_powers += 1
        TRB = B[4:6]

        block = ctx.enter_context(nc.Block())

        @block.sync
        def _(sp):
            x, pe_in = a["x"][0], a["p"][0, 0]
            for tt in range(TT):
                sp.dma_start(hres[:, tt, :], x[tt * P:(tt + 1) * P, :]).then_inc(x_loaded[tt], 16)
            for c in range(RING):
                g, half = c // 2, c % 2
                src = rows(w_in[half * 512:(half + 1) * 512, GROUP_COL[g]:GROUP_COL[g] + GROUP])
                sp.dma_start(ring[:, c, :].rearrange("p (k n) -> p k n", k=4), src).then_inc(win_loaded[c], 16)
            sp.dma_start(wide[:, :, :], rows(a["w_out"][0])).then_inc(s["wout_loaded"], 16)

            def load_item(e, before):
                for c in range(RING):
                    before(c)
                    if c < KD:
                        sp.dma_start(ring[:, c, :], w1[e, c * P:(c + 1) * P, :]).then_inc(chunk_loaded[c], 16)
                    else:
                        j = c - KD
                        sp.dma_start(ring[:, c, :].rearrange("p (k n) -> p k n", k=2),
                                     rows(w2[e, 2 * j * P:2 * (j + 1) * P, :])).then_inc(chunk_loaded[c], 16)

            load_item(0, lambda c: sp.wait_ge(s["proj_done"], 2 * (c // 2) + 2))
            sp.wait_ge(s["pv_done"], 8)
            sp.wait_ge(s["sc_done"], 8)
            sp.dma_start(b1r[0:E, :], a["b1"][0]).then_inc(s["b_loaded"], 16)
            sp.dma_start(b2r[0:E, :], a["b2"][0]).then_inc(s["b_loaded"], 16)
            sp.wait_ge(s["out_done"], 4)
            sp.dma_start(wide[:, :, :], rows(a["w_ple_gate"][0])).then_inc(s["gate_loaded"], 16)
            sp.wait_ge(s["b_used"], 1)
            sp.dma_start(wp, rows(a["w_ple_proj"][0])).then_inc(s["tail_loaded"], 16)
            sp.dma_start(pin, pe_in.rearrange("(t p) n -> p t n", p=P)).then_inc(s["tail_loaded"], 16)
            with sp.Fori(1, E) as e:
                load_item(e, lambda c: sp.wait_ge(s["chunk_used"], (e - 1) * RING + (c + 1)))
            sp.wait_ge(s["tables_ready"], 1)
            n = sp.value_load(ints[0:1, EXTRA:EXTRA + 1], min_val=0, max_val=EXTRA)
            with sp.If(n > 0):
                with sp.Fori(0, (n + 1) // 2 * 2) as i:
                    e = sp.value_load(ints[0:1, bass.ds(i, 1)], min_val=0, max_val=E - 1)
                    load_item(e, lambda c: sp.wait_ge(s["chunk_used"], (i + (E - 1)) * RING + (c + 1)))
            for q in range(4):
                tt, half = q // 2, q % 2
                sp.wait_ge(s["y_final"], q + 1)
                sp.dma_start(out[0, tt * P:(tt + 1) * P, half * 512:(half + 1) * 512],
                             xn[:, tt, half * 512:(half + 1) * 512]).then_inc(s["stored"], 16)
            sp.wait_ge(s["stored"], 64)

        @block.gpsimd
        def _(pool):
            g = nc.gpsimd
            tn = Turns(pool, s["pool_turn"])
            g.memset(mhalf, -0.5).then_inc(s["mhalf_made"], 1)
            g.memset(ident[:, :], 0.0).then_inc(s["pool_turn"], 1)
            g.memset(ones[:, :], 1.0).then_inc(s["pool_turn"], 1)
            g.memset(fmask, 0.0).then_inc(s["pool_turn"], 1)
            tn.n = 3
            pool.wait_ge(s["pool_turn"], 3)
            g.affine_select(out=ident[:, :], in_=ident[:, :], compare_op=ALU.not_equal, fill=1.0, base=0,
                            pattern=[[-1, P]], channel_multiplier=1).then_inc(s["consts_made"], 1)
            g.affine_select(out=upper[:, :], in_=ones[:, :], compare_op=ALU.is_ge, fill=0.0, base=0,
                            pattern=[[1, P]], channel_multiplier=-1).then_inc(s["consts_made"], 1)
            g.affine_select(out=fmask[:, P:T], in_=fmask[:, P:T], compare_op=ALU.is_ge, fill=NEG, base=0,
                            pattern=[[-1, P]], channel_multiplier=1).then_inc(s["consts_made"], 1)
            pool.wait_ge(s["vrow_ready"], 1)
            pool.dma_start(skew[:, :].rearrange("p (h n) -> p h n", h=DIFF_HEADS),
                           vrow).then_inc(s["skew_stored"], 16)
            pows = {"norm": [(ssq[:, tt:tt + 1], rstd[:, tt:tt + 1]) for tt in range(TT)],
                    "qk": [(ms, qr)], "sub": [(dms, dr)]}
            k = 0

            def power(src, dst):
                nonlocal k
                k += 1
                pool.wait_ge(s["mean_ready"], k)
                g.tensor_tensor(dst, src, mhalf[:, 0:src.shape[1]], ALU.pow).then_inc(s["pow_done"], 1)

            for pair in pows["norm"]:
                power(*pair)
            pool.wait_ge(s["skew_stored"], 16)
            n = DIFF_HEADS * VROW
            back = bass.AP(skew.tensor, skew.offset + P - 1, [[n - 1, P], [VROW, DIFF_HEADS], [1, T]])
            pool.dma_start(t5, back).then_inc(s["t5_loaded"], 16)
            for step, i in ORDER:
                if step == "proj" and i in QK_UNITS:
                    power(*pows["qk"][0])
                if step == "pv" and i >= 8:
                    power(*pows["sub"][0])
            for pair in pows["norm"]:
                power(*pair)
            g.iota(iota1, [[1, SLOTS]], base=1, channel_multiplier=0,
                   allow_small_or_imprecise_dtypes=True).then_inc(s["consts_made"], 1)
            g.iota(iotae, [[1, E]], base=0, channel_multiplier=0,
                   allow_small_or_imprecise_dtypes=True).then_inc(s["consts_made"], 1)
            g.iota(iota16, [[1, EXTRA]], base=0, channel_multiplier=0,
                   allow_small_or_imprecise_dtypes=True).then_inc(s["consts_made"], 1)
            g.iota(iotap, [[0, 1]], base=0, channel_multiplier=1,
                   allow_small_or_imprecise_dtypes=True).then_inc(s["consts_made"], 1)
            for pair in pows["norm"]:
                power(*pair)

        @block.scalar
        def _(act):
            c = nc.scalar
            tn = Turns(act, s["act_turn"])
            for i, name in enumerate(("g_attn", "g_mlp", "g_ple")):
                act.dma_start(grow[i * KD:(i + 1) * KD, :],
                              a[name][0].rearrange("(k p) -> k p", p=P)).then_inc(s["vec_loaded"], 16)
            act.dma_start(relb[0:BUCKETS, :], a["rel_bias"]).then_inc(s["vec_loaded"], 16)
            act.dma_start(bucket[0:BUCKETS + 1, :], a["buckets"]).then_inc(s["vec_loaded"], 16)
            act.dma_start(wf[:, :, :], rows(w_in[:, FOX_F0:FOX_F0 + 8])).then_inc(s["wf_loaded"], 16)
            act.dma_start(bf, bass.AP(a["b_f"].tensor, a["b_f"].offset, [[0, P], [1, 8]])).then_inc(s["wf_loaded"], 16)
            act.wait_ge(s["gain_ones"], 1)
            for dst, name in ((gq66[0:HD], "g_fox_q"), (gk66[0:HD], "g_fox_k"), (gq2[0:HD], "g_diff_q"),
                              (gq2[HD:P], "g_diff_q"), (gk2[0:HD], "g_diff_k"), (gk2[HD:P], "g_diff_k"),
                              (gsub, "g_subln")):
                act.dma_start(dst, a[name].rearrange("a p -> p a")).then_inc(s["head_loaded"], 16)
            for i, name in enumerate(("lambda_q1", "lambda_k1", "lambda_q2", "lambda_k2")):
                act.dma_start(lamv[:, i, :], bass.AP(a[name].tensor, a[name].offset,
                                                     [[0, P], [1, HD]])).then_inc(s["head_loaded"], 16)
            act.dma_start(wr[:, :, :], rows(a["w_router"][0])).then_inc(s["router_loaded"], 16)
            act.wait_ge(s["vrow_T"], 1)
            for h in range(DIFF_HEADS):
                ins = c.copy(vrow[:, h, :], B[2 + h][:, 0:VROW])
            ins.then_inc(s["vrow_ready"], 1)

            def sums(first):
                for tt in range(TT):
                    first(tt)
                    c.activation(junk[:, tt, :], hres[:, tt, :], ACT.Square,
                                 accum_out=ssq[:, tt:tt + 1]).then_inc(s["sums_ready"], 1)

            sums(lambda tt: act.wait_ge(x_loaded[tt], 16))
            act.wait_ge(s["lam_ready"], 1)
            c.activation(lam[:, 2:4], lam[:, 0:2], ACT.Exp).then_inc(s["lam_exp"], 1)
            act.wait_ge(s["z_ready"], 1)
            tn.link(c.activation(ze, zn, ACT.Exp))
            c.activation(ze, ze, ACT.Ln, bias=one).then_inc(s["fe_ready"], 1)

            def tr_copy(j, dst, src, scale):
                act.wait_ge(s["turned"], j + 1)
                c.activation(dst, src, ACT.Copy if isinstance(scale, float) else ACT.Identity,
                             scale=scale).then_inc(s["turned_copied"], 1)

            act.wait_ge(s["head_loaded"], 16 * 11)
            act.wait_ge(s["gain_scaled"], 1)
            j = 0
            for step, i in ORDER:
                if step == "proj":
                    act.wait_ge(s["proj_done"], i + 1)
                    if i in QK_UNITS:
                        act.wait_ge(s["mean_ready"], powers_before[step, i])
                        c.activation(sq, B[i % 2][:, :], ACT.Square).then_inc(s["sq_ready"], 1)
                    else:
                        c.copy((fv if i < 6 else dv)[:, i % 2, :], B[i % 2][:, :]).then_inc(s["v_copied"], 1)
                elif step == "qkT":
                    tt = i % 2
                    if i < 4:
                        dst, gain = (fqT, gq66) if i < 2 else (fkT, gk66)
                        for b in range(2):
                            tr_copy(j, dst[0:AUG, 4 * b:4 * b + 4, tt * P:(tt + 1) * P],
                                    TRB[j % 2][0:AUG, :].rearrange("p (h t) -> p h t", h=4), gain[0:AUG])
                            j += 1
                    else:
                        dst, gain = (dqT, gq2) if i < 8 else (dkT, gk2)
                        tr_copy(j, dst[:, :, tt * P:(tt + 1) * P],
                                TRB[j % 2][:, :].rearrange("p (h t) -> p h t", h=4), gain)
                        j += 1
                elif step == "sc":
                    act.wait_ge(s["sc_max"], i + 1)
                    w = S[i % 2]
                    c.activation(w[:, 0:P], w[:, 0:P], ACT.Exp, bias=nmax[:, i % 2, 0:1],
                                 accum_out=esum[:, i % 2, 0:1]).then_inc(s["exp_done"], 1)
                    c.activation(w[:, P:VROW], w[:, P:VROW], ACT.Exp, bias=nmax[:, i % 2, 1:2],
                                 accum_out=esum[:, i % 2, 1:2]).then_inc(s["exp_done"], 1)
                elif step == "pt":
                    if i >= 2:
                        act.wait_ge(s["pv_done"], i - 1)
                    tr_copy(j, PT[i % 2], TRB[j % 2][:, 0:VROW], 1.0)
                    j += 1
                elif step == "pv" and i >= 8:
                    act.wait_ge(s["pv_done"], i + 1)
                    act.wait_ge(s["pow_done"], powers_before[step, i])
                    for b in range(TT):
                        ins = c.activation(sq[:, b * DV:(b + 1) * DV], B[6 + i % 2][:, b * DV:(b + 1) * DV],
                                           ACT.Square, accum_out=dms[:, b:b + 1])
                        ins.then_inc(s["dsum_ready"], 1)
                elif step == "mix":
                    for tt in range(TT):
                        tr_copy(j, aT[:, 4 * i:4 * i + 4, tt * P:(tt + 1) * P],
                                TRB[j % 2][:, :].rearrange("p (h t) -> p h t", h=4), gsub if i else 1.0)
                        j += 1
            act.dma_start(brow[0:1, :], a["b_router"]).then_inc(s["router_loaded"], 16)

            def after_out(tt):
                act.wait_ge(s["res_ready"], 2 * tt + 2)
                act.wait_ge(s["out_done"], 4)

            sums(after_out)
            act.wait_ge(s["router_dve"], 1)
            for tt in range(TT):
                c.activation(e4[:, tt, :], mx8[:, tt, 0:TOPK], ACT.Exp, bias=nv0[:, tt:tt + 1],
                             accum_out=es[:, tt:tt + 1]).then_inc(s["router_act"], 1)

            act.wait_ge(s["tables_ready"], 1)
            n = act.value_load(ints[0:1, EXTRA:EXTRA + 1], min_val=0, max_val=EXTRA)
            with act.Fori(0, (n + 1) // 2 + E // 2) as p:
                act.wait_ge(s["sgt_done"], p + 1)
                c.copy(SGT, TB[:, 0:T]).then_inc(s["t_taken"], 1)
                for i in range(2):
                    act.wait_ge(s["glu_ready"], 2 * p + i + 1)
                    c.activation(sig, glu, ACT.Sigmoid, scale=ALPHA).then_inc(s["sig_ready"], 1)
                    act.wait_ge(s["chunk_used"], 2 * RING * p + (i + 1) * RING)
                    c.copy(outT[:, :, i * SLOTS:(i + 1) * SLOTS],
                           TB[:, :].rearrange("p (k c) -> p k c", k=KD)).then_inc(s["t_taken"], 1)
                act.wait_ge(s["o_done"], p + 1)
                c.copy(outs[:, 512:D], H[1][:, :]).then_inc(s["o_taken_a"], 1)

            def after_moe(tt):
                act.wait_ge(s["y_taken"], 2 * tt + 2)

            sums(after_moe)
            for q in range(4):
                act.wait_ge(s["gate_done"], q + 1)
                c.activation(ring[:, q, 0:512], Y[q][:, :], ACT.Sigmoid).then_inc(s["sg_ready"], 1)

        @block.tensor
        def _(pe):
            mm, tr = nc.tensor.matmul, nc.tensor.transpose
            pe.wait_ge(s["consts_made"], 2)
            pe.wait_ge(s["vec_loaded"], 16 * 5)
            tr(B[0][:, 0:3 * KD], grow[0:3 * KD, :], ident[0:3 * KD, 0:3 * KD]).then_inc(s["gcols_T"], 1)
            pe.wait_ge(s["masked_bucket"], 1)
            for h in range(DIFF_HEADS):
                ins = mm(B[2 + h][:, 0:VROW], spread(relb[0:BUCKETS + 1, h], 1, P), bucket[0:BUCKETS + 1, :],
                         start=True, stop=True)
            ins.then_inc(s["vrow_T"], 1)

            def turn_x(k, banks, first):
                for tt in range(TT):
                    pe.wait_ge(s["xn_ready"], TT * k + tt + 1)
                    for b in range(2):
                        first(2 * tt + b)
                        for j in range(4):
                            ins = tr(banks[2 * tt + b][:, j * P:(j + 1) * P],
                                     xn[:, tt, (4 * b + j) * P:(4 * b + j + 1) * P], ident[:, :])
                        ins.then_inc(s["xT_done"], 1)

            turn_x(0, B[2:6], lambda q: pe.wait_ge(s["vrow_ready"], 1))
            pe.wait_ge(s["wf_loaded"], 32)
            for tt in range(TT):
                pe.wait_ge(s["xT_ready"], 2 * tt + 2)
                for k in range(KD):
                    ins = mm(B[6][:, 8 * tt:8 * tt + 8], aT[:, k, tt * P:(tt + 1) * P], wf[:, k, :],
                             start=(k == 0), stop=(k == KD - 1))
            ins.then_inc(s["f_done"], 1)

            j = 0

            def bank_turn():
                if j >= 2:
                    pe.wait_ge(s["turned_copied"], j - 1)
                return TRB[j % 2]

            for step, i in ORDER:
                if step == "proj":
                    g, tt = i // 2, i % 2
                    if i == 0:
                        pe.wait_ge(s["gcols_ready"], 1)
                    if i >= 2:
                        unit_free(pe, i - 2)
                    for k in range(KD):
                        if k % 4 == 0:
                            pe.wait_ge(win_loaded[2 * g + k // 4], 16)
                        ins = mm(B[i % 2][:, :], aT[:, k, tt * P:(tt + 1) * P],
                                 ring[:, 2 * g + k // 4, (k % 4) * GROUP:(k % 4 + 1) * GROUP],
                                 start=(k == 0), stop=(k == KD - 1))
                    ins.then_inc(s["proj_done"], 1)
                elif step == "cum":
                    pe.wait_ge(s["logf_ready"], 1)
                    mm(B[7][:, 0:8], upper[:, :], logf[:, 0, :], start=True, stop=True)
                    mm(B[7][:, 8:16], ones[:, :], logf[:, 0, :], start=True, stop=False)
                    mm(B[7][:, 8:16], upper[:, :], logf[:, 1, :], start=False, stop=True).then_inc(s["cum_done"], 1)
                elif step == "qkT":
                    pe.wait_ge(s["qk_ready" if i < 4 else "qk_scaled"], QK_UNITS.index(i) + 1)
                    if i < 4:
                        for b in range(2):
                            bank = bank_turn()
                            for h in range(4):
                                ins = tr(bank[0:AUG, h * P:(h + 1) * P], qkn[i % 2][:, 4 * b + h, :], ident[:, :])
                            ins.then_inc(s["turned"], 1)
                            j += 1
                    else:
                        bank = bank_turn()
                        for h in range(4):
                            ins = tr(bank[:, h * P:(h + 1) * P], qkn_flat[i % 2][:, h * P:(h + 1) * P], ident[:, :])
                        ins.then_inc(s["turned"], 1)
                        j += 1
                elif step == "sc":
                    bank = B[2 + i % 2]
                    if i == 0:
                        pe.wait_ge(s["turned_copied"], 8)
                    if i == 8:
                        pe.wait_ge(s["turned_copied"], turned_after["qkT", 9])
                    if i >= 2:
                        pe.wait_ge(s["sc_masked"], i - 1)
                    if i < 8:
                        q, k = fqT[0:AUG, i, :], fkT[0:AUG, i, :]
                    else:
                        h, m = (i - 8) // 2, i % 2
                        q, k = dqT[m * HD:(m + 1) * HD, h, :], dkT[m * HD:(m + 1) * HD, h, :]
                    mm(bank[:, 0:P], q[:, 0:P], k[:, 0:P], start=True, stop=True)
                    mm(bank[:, P:VROW], q[:, P:T], k[:, :], start=True, stop=True).then_inc(s["sc_done"], 1)
                elif step == "pt":
                    if i < 8:
                        pe.wait_ge(s["exp_done"], 2 * i + 2)
                    else:
                        pe.wait_ge(s["comb_ready"], i - 7)
                    bank, w = bank_turn(), S[i % 2 if i < 8 else 0]
                    for b in range(3):
                        ins = tr(bank[:, b * P:(b + 1) * P], w[:, b * P:(b + 1) * P], ident[:, :])
                    ins.then_inc(s["turned"], 1)
                    j += 1
                elif step == "pv":
                    bank, w = B[6 + i % 2], PT[i % 2]
                    pe.wait_ge(s["turned_copied"], turned_after["pt", i])
                    if i >= 2:
                        pe.wait_ge(s["pv_taken"], i - 1)
                    if i < 8:
                        v, n = [fv[:, t, i * HD:(i + 1) * HD] for t in range(TT)], HD
                    else:
                        v, n = [dv[:, t, (i - 8) * DV:(i - 7) * DV] for t in range(TT)], DV
                    if i in (0, 8):
                        pe.wait_ge(s["v_copied"], 2 if i < 8 else 4)
                    mm(bank[:, 0:n], w[:, 0:P], v[0], start=True, stop=True)
                    mm(bank[:, n:2 * n], w[:, P:T], v[0], start=True, stop=False)
                    mm(bank[:, n:2 * n], w[:, T:VROW], v[1], start=False, stop=True).then_inc(s["pv_done"], 1)
                elif step == "mix":
                    pe.wait_ge(s["pv_taken"], 12 if i else 8)
                    for tt in range(TT):
                        bank = bank_turn()
                        for b in range(4):
                            ins = tr(bank[:, b * P:(b + 1) * P], xn[:, tt, (4 * i + b) * P:(4 * i + b + 1) * P],
                                     ident[:, :])
                        ins.then_inc(s["turned"], 1)
                        j += 1
            pe.wait_ge(s["wout_loaded"], 16)
            pe.wait_ge(s["turned_copied"], j)
            for q, bank in enumerate((B[0], B[1], B[2], B[3])):
                tt, half = q // 2, q % 2
                for k in range(KD):
                    ins = mm(bank[:, :], aT[:, k, tt * P:(tt + 1) * P], wide[:, k, half * 512:(half + 1) * 512],
                             start=(k == 0), stop=(k == KD - 1))
                ins.then_inc(s["out_done"], 1)
            turn_x(1, B[4:8], lambda q: None)
            pe.wait_ge(s["router_loaded"], 32)
            pe.wait_ge(s["res_ready"], 4)
            for tt in range(TT):
                pe.wait_ge(s["xT_ready"], 4 + 2 * tt + 2)
                for k in range(KD):
                    mm(B[0][:, tt * E:(tt + 1) * E], aT[:, k, tt * P:(tt + 1) * P], wr[:, k, :],
                       start=(k == 0), stop=False)
                ins = mm(B[0][:, tt * E:(tt + 1) * E], ones[0:1, :], brow[0:1, :], start=False, stop=True)
            ins.then_inc(s["router_pe"], 1)
            pe.wait_ge(s["router_dve"], 2)
            mm(B[1][:, 0:E], upper[:, :], M[:, 0, :], start=True, stop=True)
            mm(B[1][:, E:2 * E], ones[:, :], M[:, 0, :], start=True, stop=False)
            mm(B[1][:, E:2 * E], upper[:, :], M[:, 1, :], start=False, stop=True)
            mm(B[1][0:E, 2 * E:2 * E + 1], M[:, 0, :], ones[:, 0:1], start=True, stop=False)
            mm(B[1][0:E, 2 * E:2 * E + 1], M[:, 1, :], ones[:, 0:1], start=False, stop=True) \
                .then_inc(s["router_pe"], 1)
            pe.wait_ge(s["router_dve"], 3)
            for q, src in enumerate((P1, G)):
                for tt in range(TT):
                    ins = tr(B[2][0:E, q * T + tt * P:q * T + (tt + 1) * P], src[:, tt, :], ident[:, :])
            ins.then_inc(s["router_pe"], 1)
            mm(B[3][0:E, 0:1], upper[0:E, 0:E], extra[0:E, :], start=True, stop=True)
            mm(B[3][0:1, 1:2], ones[0:E, 0:1], extra[0:E, :], start=True, stop=True).then_inc(s["router_pe"], 1)
            pe.wait_ge(s["router_dve"], 4)
            for tt in range(TT):
                mm(B[4][:, tt * COLS:(tt + 1) * COLS], P1T[0:E, tt * P:(tt + 1) * P], Eall[0:E, :],
                   start=True, stop=False)
                mm(B[4][:, tt * COLS:(tt + 1) * COLS], ones[0:E, :], Bneg[0:E, :], start=False, stop=True)
                mm(B[4][:, (TT + tt) * COLS:(TT + tt + 1) * COLS], GT[0:E, tt * P:(tt + 1) * P], Eall[0:E, :],
                   start=True, stop=True)
            mm(B[5][0:1, 0:EXTRA], iotap[0:E, :], Eall[0:E, E:ITEMS], start=True, stop=True) \
                .then_inc(s["router_pe"], 1)
            pe.wait_ge(s["b_loaded"], 32)
            for n in range(KD):
                for g in range(2):
                    ins = mm(B[6 + g][:, n * COLS:(n + 1) * COLS],
                             b1r[0:E, 2 * n * P + g:2 * (n + 1) * P:2], Eall[0:E, :], start=True, stop=True)
            ins.then_inc(s["router_pe"], 1)
            for q in range(4):
                tt, half = q // 2, q % 2
                ins = mm(Y[q][:, :], GT[0:E, tt * P:(tt + 1) * P], b2r[0:E, half * 512:(half + 1) * 512],
                         start=True, stop=False, skip_group_check=True)
            ins.then_inc(s["b_used"], 1)

            def gather(i):
                for k in range(KD):
                    for tt in range(TT):
                        ins = mm(GB[:, k * SLOTS:(k + 1) * SLOTS], xn[:, tt, k * P:(k + 1) * P], Sel[:, tt, :],
                                 start=(k == 0 and tt == 0), stop=(tt == 1), skip_group_check=True)
                ins.then_inc(s["gath_done"], 1)

            pe.wait_ge(s["tables_ready"], 1)
            pe.wait_ge(s["sel_ready"], 1)
            gather(0)
            n = pe.value_load(ints[0:1, EXTRA:EXTRA + 1], min_val=0, max_val=EXTRA)
            with pe.Fori(0, (n + 1) // 2 + E // 2) as p:
                for i in range(2):
                    pe.wait_ge(s["gath_taken"], 2 * p + i + 1)
                    if i:
                        pe.wait_ge(s["h_taken"], 2 * p + 1)
                    for k in range(KD):
                        pe.wait_ge(chunk_loaded[k], (2 * p + (i + 1)) * 16)
                        for f in range(KD):
                            for g in range(2):
                                ins = mm(H[g][:, f * SLOTS:(f + 1) * SLOTS],
                                         ring[:, k, 2 * f * P + g:2 * (f + 1) * P:2], xsel[i][:, k, :],
                                         start=(k == 0 and f == 0), stop=(k == KD - 1), skip_group_check=True)
                        ins.then_inc(s["chunk_used"], 1)
                    if i == 0:
                        pe.wait_ge(s["sel_ready"], 2 * p + 2)
                        for tt in range(TT):
                            ins = tr(TB[:, tt * P:(tt + 1) * P], SG[:, tt, :], ident[:, :])
                        ins.then_inc(s["sgt_done"], 1)
                    if i:
                        pe.wait_ge(s["sel_ready"], 2 * p + 3)
                    gather(i)
                    pe.wait_ge(s["t_taken"], 3 * p + (i + 1))
                    pe.wait_ge(s["hT_ready"], 2 * p + (i + 1))
                    for k in range(KD):
                        c = KD + k // 2
                        if k % 2 == 0:
                            pe.wait_ge(chunk_loaded[c], (2 * p + (i + 1)) * 16)
                        for m in range(KD):
                            ins = mm(TB[:, m * SLOTS:(m + 1) * SLOTS],
                                     ring[:, c, (k % 2) * D + m * P:(k % 2) * D + (m + 1) * P], hT[i][:, k, :],
                                     start=(k == 0 and m == 0), stop=(k == KD - 1), skip_group_check=True)
                        if k % 2:
                            ins.then_inc(s["chunk_used"], 1)
                pe.wait_ge(s["h_taken"], 2 * p + 2)
                pe.wait_ge(s["t_taken"], 3 * p + 3)
                for k in range(KD):
                    ins = tr(H[k // 4][:, (k % 4) * P:(k % 4 + 1) * P], outT[:, k, :], ident[:, :])
                ins.then_inc(s["o_done"], 1)
                pe.wait_ge(s["o_taken_v"], p + 1)
                pe.wait_ge(s["o_taken_a"], p + 1)
                for q in range(4):
                    tt, half = q // 2, q % 2
                    ins = mm(Y[q][:, :], SGT[:, tt * P:(tt + 1) * P], outs[:, half * 512:(half + 1) * 512],
                             start=False, stop=False, skip_group_check=True)
                ins.then_inc(s["comb_done"], 1)
            pe.wait_ge(s["tail_loaded"], 32)
            for k in range(2):
                for tt in range(TT):
                    ins = tr(GB[:, k * T + tt * P:k * T + (tt + 1) * P], pin[:, tt, k * P:(k + 1) * P], ident[:, :])
            ins.then_inc(s["pT_done"], 1)
            pe.wait_ge(s["pT_ready"], 1)
            for q in range(4):
                tt, half = q // 2, q % 2
                for k in range(2):
                    ins = mm(B[4 + q][:, :], pT[:, k, tt * P:(tt + 1) * P], wp[:, k, half * 512:(half + 1) * 512],
                             start=(k == 0), stop=(k == 1))
            ins.then_inc(s["pp_done"], 1)
            turn_x(2, Y, lambda q: pe.wait_ge(s["y_taken"], q + 1))
            pe.wait_ge(s["gate_loaded"], 16)
            for q in range(4):
                tt, half = q // 2, q % 2
                pe.wait_ge(s["xT_ready"], 8 + max(q + 1, 2 * tt + 2))
                for k in range(KD):
                    ins = mm(Y[q][:, :], aT[:, k, tt * P:(tt + 1) * P], wide[:, k, half * 512:(half + 1) * 512],
                             start=(k == 0), stop=(k == KD - 1))
                ins.then_inc(s["gate_done"], 1)

        @block.vector
        def _(dve):
            v = nc.vector
            tn = Turns(dve, s["dve_turn"])
            v.memset(gains, 1.0).then_inc(s["gain_ones"], 1)
            v.memset(relb[BUCKETS:BUCKETS + 1, :], NEG).then_inc(s["masked_bucket"], 1)
            dve.wait_ge(s["gcols_T"], 1)
            v.tensor_copy(gcols[:, :], B[0][:, 0:3 * KD]).then_inc(s["gcols_ready"], 1)
            dve.wait_ge(s["gcols_ready"], 1)
            n_pow, n_x = 0, 0

            def request(ins):
                nonlocal n_pow
                n_pow += 1
                ins.then_inc(s["mean_ready"], 1)

            def mean(dst, src, n):
                request(v.tensor_scalar(dst, src, 1.0 / n, EPS, ALU.mult, ALU.add))

            def norm(k, banks, between):
                for tt in range(TT):
                    dve.wait_ge(s["sums_ready"], TT * k + tt + 1)
                    mean(ssq[:, tt:tt + 1], ssq[:, tt:tt + 1], D)
                first = n_pow - TT
                for tt in range(TT):
                    dve.wait_ge(s["pow_done"], first + tt + 1)
                    v.tensor_scalar(xn[:, tt, :], hres[:, tt, :], rstd[:, tt:tt + 1], None,
                                    ALU.mult).then_inc(s["xn_ready"], 1)
                between()
                for q in range(4):
                    tt, b = q // 2, q % 2
                    dve.wait_ge(s["xT_done"], 4 * k + q + 1)
                    v.tensor_tensor(aT[:, 4 * b:4 * b + 4, tt * P:(tt + 1) * P],
                                    banks[q][:, :].rearrange("p (k t) -> p k t", k=4),
                                    spread(gcols[:, KD * k + 4 * b:KD * k + 4 * b + 4], 2, P),
                                    ALU.mult).then_inc(s["xT_ready"], 1)

            def head_constants():
                dve.wait_ge(s["head_loaded"], 16 * 11)
                tn.link(v.tensor_tensor(lamp, lamv[:, 0:4:2, :], lamv[:, 1:4:2, :], ALU.mult))
                v.tensor_reduce(lam[:, 0:2], lamp, X, ALU.add).then_inc(s["lam_ready"], 1)
                v.tensor_scalar(gq66[0:HD], gq66[0:HD], HD ** -0.5, None, ALU.mult)
                v.tensor_scalar(gq2, gq2, HD ** -0.5, None, ALU.mult)
                v.tensor_scalar(gsub, gsub, 1.0 - LAM_INIT, None, ALU.mult).then_inc(s["gain_scaled"], 1)

            norm(0, B[2:6], head_constants)
            dve.wait_ge(s["lam_exp"], 1)
            tn.link(v.tensor_tensor(lam[:, 4:5], lam[:, 3:4], lam[:, 2:3], ALU.subtract))
            tn.link(v.tensor_scalar(lam[:, 5:6], lam[:, 4:5], -LAM_INIT, None, ALU.add))
            dve.wait_ge(s["f_done"], 1)
            dve.wait_ge(s["wf_loaded"], 32)
            tn.link(v.tensor_tensor(z, B[6][:, 0:16].rearrange("p (t h) -> p t h", t=TT), spread(bf, 1, TT),
                                    ALU.add))
            tn.link(v.tensor_scalar(zn, z, -1.0, None, ALU.mult))
            v.tensor_tensor(zn, z, zn, ALU.min).then_inc(s["z_ready"], 1)
            tn.link(v.tensor_scalar(zlow, z, 0.0, None, ALU.min))
            dve.wait_ge(s["fe_ready"], 1)
            v.tensor_tensor(logf, zlow, ze, ALU.subtract).then_inc(s["logf_ready"], 1)

            n_x = 0
            for step, i in ORDER:
                if step == "cum":
                    dve.wait_ge(s["cum_done"], 1)
                    c = B[7][:, 0:16].rearrange("p (t h) -> p t h", t=TT)
                    v.tensor_copy(cpos, c)
                    tn.link(v.tensor_scalar(cneg, c, -1.0, None, ALU.mult))
                elif step == "proj" and i in QK_UNITS:
                    u = QK_UNITS.index(i)
                    dve.wait_ge(s["sq_ready"], u + 1)
                    tn.link(v.tensor_reduce(ms, sq.rearrange("p (h d) -> p h d", h=8), X, ALU.add))
                    mean(ms, ms, HD)
                    dve.wait_ge(s["pow_done"], n_pow)
                    if i in (2, 3, 6, 7, 8, 9):
                        dve.wait_ge(s["turned"], turned_after["qkT", QK_UNITS[u - 2]])
                    dst = qkn[i % 2][:, :, 0:HD] if i < 4 else qkn_flat[i % 2].rearrange("p (h d) -> p h d", h=8)
                    v.tensor_tensor(dst, B[i % 2][:, :].rearrange("p (h d) -> p h d", h=8), spread(qr, 2, HD),
                                    ALU.mult).then_inc(s["qk_scaled"], 1)
                elif step == "qkT" and i < 4:
                    w, tt = qkn[i % 2], i % 2
                    gate, plain = (HD, HD + 1) if i < 2 else (HD + 1, HD)
                    v.tensor_copy(w[:, :, gate], (cpos if i < 2 else cneg)[:, tt, :])
                    v.memset(w[:, :, plain], 1.0).then_inc(s["qk_ready"], 1)
                elif step == "sc":
                    w, bank = S[i % 2], B[2 + i % 2]
                    dve.wait_ge(s["sc_done"], i + 1)
                    if 2 <= i < 10:
                        dve.wait_ge(s["turned"], turned_after["pt", i - 2])
                    elif i >= 10:
                        dve.wait_ge(s["turned"], turned_after["pt", i // 2 + 3])
                    if i == 0:
                        dve.wait_ge(s["consts_made"], 3)
                    if i == 8:
                        dve.wait_ge(s["t5_loaded"], 16)
                    bias = fmask if i < 8 else t5[:, (i - 8) // 2, :]
                    v.tensor_tensor(w[:, 0:P], bank[:, 0:P], bias[:, P:T], ALU.add)
                    v.tensor_tensor(w[:, P:VROW], bank[:, P:VROW], bias, ALU.add).then_inc(s["sc_masked"], 1)
                    dve.wait_ge(s["sc_masked"], i + 1)
                    v.tensor_reduce(nmax[:, i % 2, 0:1], w[:, 0:P], X, ALU.max, negate=True)
                    v.tensor_reduce(nmax[:, i % 2, 1:2], w[:, P:VROW], X, ALU.max,
                                    negate=True).then_inc(s["sc_max"], 1)
                elif step == "pt" and i < 8:
                    dve.wait_ge(s["exp_done"], 2 * i + 2)
                    tn.link(v.reciprocal(rsum[:, i % 2, :], esum[:, i % 2, :]))
                elif step == "pt":
                    dve.wait_ge(s["exp_done"], 4 * (i - 8) + 20)
                    tn.link(v.reciprocal(rsum, esum))
                    v.tensor_scalar(nl, rsum[:, 1, :], lam[:, 5:6], None, ALU.mult)
                    v.tensor_scalar(S[0][:, 0:P], S[0][:, 0:P], rsum[:, 0, 0:1], None, ALU.mult)
                    tn.link(v.tensor_scalar(S[0][:, P:VROW], S[0][:, P:VROW], rsum[:, 0, 1:2], None, ALU.mult))
                    v.scalar_tensor_tensor(out=S[0][:, 0:P], in0=S[1][:, 0:P], scalar=nl[:, 0:1],
                                           in1=S[0][:, 0:P], op0=ALU.mult, op1=ALU.add)
                    v.scalar_tensor_tensor(out=S[0][:, P:VROW], in0=S[1][:, P:VROW], scalar=nl[:, 1:2],
                                           in1=S[0][:, P:VROW], op0=ALU.mult,
                                           op1=ALU.add).then_inc(s["comb_ready"], 1)
                    dve.wait_ge(s["comb_ready"], i - 7)
                elif step == "pv":
                    bank, n = B[6 + i % 2], HD if i < 8 else DV
                    if i < 8:
                        dve.wait_ge(s["pv_done"], i + 1)
                        r, c0 = rsum[:, i % 2, :], i * HD
                    else:
                        dve.wait_ge(s["dsum_ready"], 2 * (i - 8) + 2)
                        mean(dms, dms, DV)
                        dve.wait_ge(s["pow_done"], n_pow)
                        r, c0 = dr, 512 + (i - 8) * DV
                    v.tensor_tensor(xn[:, :, c0:c0 + n], bank[:, 0:2 * n].rearrange("p (t d) -> p t d", t=TT),
                                    spread(r, 2, n), ALU.mult).then_inc(s["pv_taken"], 1)
                    dve.wait_ge(s["pv_taken"], i + 1)

            for q in range(4):
                tt, half = q // 2, q % 2
                dve.wait_ge(s["out_done"], q + 1)
                h = hres[:, tt, half * 512:(half + 1) * 512]
                v.tensor_tensor(h, B[q][:, :], h, ALU.add).then_inc(s["res_ready"], 1)
            norm(1, B[4:8], lambda: None)

            dve.wait_ge(s["router_pe"], 1)
            tn.link(v.tensor_copy(lg, B[0][:, 0:TT * E].rearrange("p (t e) -> p t e", t=TT)))
            for tt in range(TT):
                ins = v.max(mx8[:, tt, :], lg[:, tt, :])
            tn.link(ins)
            v.tensor_scalar(nv0, mx8[:, :, 0], -1.0, None, ALU.mult).then_inc(s["router_dve"], 1)
            for tt in range(TT):
                ins = v.max_index(idx8[:, tt, :], mx8[:, tt, :], lg[:, tt, :])
            tn.link(ins)
            tn.link(v.tensor_copy(idxf, idx8[:, :, :]))
            dve.wait_ge(s["consts_made"], 7)
            tn.link(v.tensor_tensor(oh, spread(spread(iotae, 1, TOPK), 1, TT), spread(idxf[:, :, 0:TOPK], 3, E),
                                    ALU.is_equal))
            v.tensor_reduce(M, oh.rearrange("p t j e -> p t e j"), X, ALU.add).then_inc(s["router_dve"], 1)
            dve.wait_ge(s["router_act"], TT)
            tn.link(v.reciprocal(es, es))
            tn.link(v.tensor_tensor(e4, e4, spread(es, 2, TOPK), ALU.mult))
            tn.link(v.tensor_tensor(ohg, oh, spread(e4, 3, E), ALU.mult))
            v.tensor_reduce(G, ohg.rearrange("p t j e -> p t e j"), X, ALU.add)
            dve.wait_ge(s["router_pe"], 2)
            dve.wait_ge(s["router_dve"], 2)
            v.tensor_tensor(P1, B[1][:, 0:TT * E].rearrange("p (t e) -> p t e", t=TT), M, ALU.mult)
            tn.link(v.tensor_copy(cnt[0:E], B[1][0:E, 2 * E:2 * E + 1]))
            for r in range(MORE):
                ins = v.tensor_scalar(over[0:E, r:r + 1], cnt[0:E], float(SLOTS * (r + 1)), None, ALU.is_gt)
            tn.link(ins)
            v.tensor_reduce(extra[0:E], over[0:E], X, ALU.add).then_inc(s["router_dve"], 1)
            v.memset(Eall[0:E], 0.0)
            tn.link(v.memset(Bneg[0:E], 0.0))
            v.tensor_copy(Eall[0:E, 0:E], ident[0:E, 0:E])
            dve.wait_ge(s["router_dve"], 3)
            dve.wait_ge(s["router_pe"], 4)
            v.tensor_copy(arena[0:E, 0:2 * T], B[2][0:E, :])
            v.tensor_copy(ints[0:1, EXTRA:EXTRA + 1], B[3][0:1, 1:2])
            tn.link(v.tensor_tensor(offs[0:E, 0:1], B[3][0:E, 0:1], extra[0:E], ALU.subtract))
            for r in range(1, MORE):
                ins = v.tensor_scalar(offs[0:E, r:r + 1], offs[0:E, 0:1], float(r), None, ALU.add)
            tn.link(ins)
            for r in range(MORE):
                ins = v.tensor_scalar(Er[0:E, r, :], iota16[0:E], offs[0:E, r:r + 1], over[0:E, r:r + 1],
                                      ALU.is_equal, ALU.mult)
            tn.link(ins)
            tail, base = Eall[0:E, E:ITEMS], Bneg[0:E, E:ITEMS]
            for r in range(MORE):
                tn.link(v.tensor_tensor(tail, tail, Er[0:E, r, :], ALU.add))
                ins = v.scalar_tensor_tensor(out=base, in0=Er[0:E, r, :], scalar=-float(SLOTS * (r + 1)), in1=base,
                                             op0=ALU.mult, op1=ALU.add)
                if r < MORE - 1:
                    tn.link(ins)
            ins.then_inc(s["router_dve"], 1)
            dve.wait_ge(s["router_pe"], 5)
            v.tensor_copy(P1i, B[4][:, 0:TT * COLS].rearrange("p (t i) -> p t i", t=TT))
            v.tensor_copy(Gi, B[4][:, TT * COLS:2 * TT * COLS].rearrange("p (t i) -> p t i", t=TT))
            v.tensor_copy(ints[0:1, 0:EXTRA], B[5][0:1, 0:EXTRA])
            dve.wait_ge(s["router_pe"], 6)
            for g in range(2):
                ins = v.tensor_copy(b1i[:, g * KD:(g + 1) * KD, :],
                                    B[6 + g][:, 0:KD * COLS].rearrange("p (k i) -> p k i", k=KD))
            ins.then_inc(s["tables_ready"], 1)
            dve.wait_ge(s["tables_ready"], 1)

            def select(i, half):
                tn.link(v.tensor_tensor(Sel, spread(iota1, 1, TT), P1i[:, :, bass.ds(i, 1)].to_broadcast((P, TT, SLOTS)),
                                        ALU.is_equal))
                v.tensor_tensor(SG[:, :, half * SLOTS:(half + 1) * SLOTS], Sel,
                                Gi[:, :, bass.ds(i, 1)].to_broadcast((P, TT, SLOTS)),
                                ALU.mult).then_inc(s["sel_ready"], 1)

            def take_tokens(half):
                v.tensor_tensor(xsel[half], GB[:, :].rearrange("p (k c) -> p k c", k=KD),
                                spread(gcols[:, KD:2 * KD], 2, SLOTS), ALU.mult).then_inc(s["gath_taken"], 1)

            select(0, 0)
            dve.wait_ge(s["gath_done"], 1)
            take_tokens(0)
            n = dve.value_load(ints[0:1, EXTRA:EXTRA + 1], min_val=0, max_val=EXTRA)
            pairs = (n + 1) // 2 + E // 2
            before, per = tn.n, 8
            with dve.Fori(0, pairs) as p:
                tn.base, tn.n = p * per + before, 0
                select(2 * p + 1, 1)
                for i in range(2):
                    b1 = [b1i[:, g * KD:(g + 1) * KD, bass.ds(2 * p + i, 1)].to_broadcast((P, KD, SLOTS))
                          for g in range(2)]
                    dve.wait_ge(s["chunk_used"], 2 * RING * p + (i * RING + KD))
                    tn.link(v.tensor_tensor(glu, H[0][:, :].rearrange("p (k c) -> p k c", k=KD), b1[0], ALU.add))
                    v.tensor_scalar(glu, glu, LIMIT, None, ALU.min).then_inc(s["glu_ready"], 1)
                    v.tensor_tensor(lin, H[1][:, :].rearrange("p (k c) -> p k c", k=KD), b1[1],
                                    ALU.add).then_inc(s["h_taken"], 1)
                    dve.wait_ge(s["h_taken"], 2 * p + (i + 1))
                    tn.link(v.tensor_scalar(lin, lin, -LIMIT, LIMIT, ALU.max, ALU.min))
                    tn.link(v.scalar_tensor_tensor(out=prod.rearrange("p k c -> p (k c)"),
                                                   in0=lin.rearrange("p k c -> p (k c)"), scalar=1.0,
                                                   in1=glu.rearrange("p k c -> p (k c)"), op0=ALU.add, op1=ALU.mult))
                    dve.wait_ge(s["sig_ready"], 2 * p + (i + 1))
                    v.tensor_tensor(hT[i], prod, sig, ALU.mult).then_inc(s["hT_ready"], 1)
                    dve.wait_ge(s["gath_done"], 2 * p + (i + 2))
                    take_tokens(1 - i)
                    if i == 0:
                        dve.wait_ge(s["sgt_done"], p + 1)
                        select(2 * p + 2, 0)
                dve.wait_ge(s["o_done"], p + 1)
                v.tensor_copy(outs[:, 0:512], H[0][:, :]).then_inc(s["o_taken_v"], 1)
                assert tn.n == per

            dve.wait_ge(s["comb_done"], pairs)
            for q in range(4):
                tt, half = q // 2, q % 2
                h = hres[:, tt, half * 512:(half + 1) * 512]
                v.tensor_tensor(h, Y[q][:, :], h, ALU.add).then_inc(s["y_taken"], 1)

            def embedding():
                dve.wait_ge(s["pT_done"], 1)
                v.tensor_copy(pT, GB[:, :].rearrange("p (k t) -> p k t", k=2)).then_inc(s["pT_ready"], 1)

            embedding()
            norm(2, Y, lambda: None)
            dve.wait_ge(s["pp_done"], 1)
            for q in range(4):
                tt, half = q // 2, q % 2
                g = ring[:, q, 0:512]
                dve.wait_ge(s["sg_ready"], q + 1)
                v.tensor_tensor(g, B[4 + q][:, :], g, ALU.mult).then_inc(s["gated"], 1)
                dve.wait_ge(s["gated"], q + 1)
                v.tensor_tensor(xn[:, tt, half * 512:(half + 1) * 512], g,
                                hres[:, tt, half * 512:(half + 1) * 512], ALU.add).then_inc(s["y_final"], 1)


INPUTS = ["x", "p", "rel_bias", "g_attn", "w_in", "b_f", "g_fox_q", "g_fox_k", "g_diff_q", "g_diff_k",
          "lambda_q1", "lambda_k1", "lambda_q2", "lambda_k2", "g_subln", "w_out", "g_mlp", "w_router", "b_router",
          "w1", "b1", "w2", "b2", "g_ple", "w_ple_gate", "w_ple_proj"]


def bucket_table():
    table = np.zeros((BUCKETS + 1, VROW), np.float32)
    exact = BUCKETS // 2
    for n in range(VROW):
        rel = 2 * P - 1 - n
        if rel < 0:
            bucket = BUCKETS
        elif rel < exact:
            bucket = rel
        else:
            bucket = min(BUCKETS - 1, exact + int(np.log(rel / exact) / np.log(P / exact) * (BUCKETS - exact) + 1e-9))
        table[bucket, n] = 1.0
    return table


def kernel(**inputs):
    import concourse.bacc as bacc
    from concourse.bass_utils import run_bass_kernel_spmd as run

    nc = bacc.Bacc("TRN2", target_bir_lowering=False, num_devices=1)
    arrays, args = {}, {}
    named = {name: np.asarray(inputs[name]) for name in INPUTS}
    named["buckets"] = bucket_table()
    for name, v in named.items():
        arrays[f"in_{name}"] = v
        args[name] = nc.dram_tensor(f"in_{name}", v.shape, mybir.dt.from_np(v.dtype), kind="ExternalInput").ap()
    out = nc.dram_tensor("out_dram", (1, T, D), F32, kind="ExternalOutput").ap()
    build(nc, args, out)
    return run(nc, [arrays], core_ids=[0]).results[0]["out_dram"]
```

```python
import numpy as np
import concourse.bass as bass
from concourse import mybir
from concourse.alu_op_type import AluOpType as ALU
from contextlib import ExitStack

F32 = mybir.dt.float32
I32 = mybir.dt.int32
U32 = mybir.dt.uint32
ACT = mybir.ActivationFunctionType
X = mybir.AxisListType.X

P = 128
T = 256
TT = T // P
D = 1024
KD = D // P
FOX_HEADS, DIFF_HEADS, HD, DV = 8, 4, 64, 128
AUG = HD + 2
FOX_F0 = 3 * FOX_HEADS * HD
GROUP = 512
GROUP_COL = [0, 512, 1024, FOX_F0 + 8, FOX_F0 + 520, FOX_F0 + 1032]
UNITS = 12
QK_UNITS = [0, 1, 2, 3, 6, 7, 8, 9]
V_UNITS = [4, 5, 10, 11]
EPS = 1e-6
NEG = -1e30
LAM_INIT = 0.8 - 0.6 * 1.0
ALPHA, LIMIT = 1.702, 7.0
BUCKETS, VROW = 32, 384

E = 32
TOPK = 4
SLOTS = 64
MORE = T // SLOTS - 1
EXTRA = T * TOPK // SLOTS
ITEMS = E + EXTRA
COLS = ITEMS + 2
RING = 12
CH = 2048

ORDER = ([("proj", 0), ("cum", 0)]
         + [s for u in range(1, 5) for s in (("proj", u), ("qkT", u - 1))]
         + [("proj", 5), ("sc", 0), ("sc", 1)]
         + [("proj", 6), ("pt", 0), ("pt", 1), ("sc", 2), ("sc", 3)]
         + [("proj", 7), ("qkT", 6), ("pv", 0), ("pv", 1), ("pt", 2), ("pt", 3), ("sc", 4), ("sc", 5)]
         + [("proj", 8), ("qkT", 7), ("pv", 2), ("pv", 3), ("pt", 4), ("pt", 5), ("sc", 6), ("sc", 7)]
         + [("proj", 9), ("qkT", 8), ("pv", 4), ("pv", 5), ("pt", 6), ("pt", 7)]
         + [("proj", 10), ("qkT", 9), ("pv", 6), ("pv", 7), ("sc", 8), ("sc", 9)]
         + [("proj", 11), ("pt", 8), ("sc", 10), ("sc", 11)]
         + [("mix", 0), ("pt", 9), ("sc", 12), ("sc", 13), ("pv", 8), ("pt", 10), ("sc", 14), ("sc", 15), ("pv", 9),
            ("pt", 11), ("pv", 10), ("pv", 11), ("mix", 1)])


def spread(ap, axis, n):
    dims = [list(d) for d in ap.ap]
    dims.insert(axis, [0, n])
    return bass.AP(ap.tensor, ap.offset, dims)


class Turns:

    def __init__(self, eng, sem):
        self.eng, self.sem, self.n, self.base = eng, sem, 0, 0

    def step(self, ins):
        ins.then_inc(self.sem, 1)
        self.n += 1

    def link(self, ins):
        self.step(ins)
        self.eng.wait_ge(self.sem, self.base + self.n)


def build(nc, a, out):
    with ExitStack() as ctx:
        def sb(name, shape, dt=F32):
            return ctx.enter_context(nc.sbuf_tensor(name, shape, dt))

        def sem(name):
            return ctx.enter_context(nc.semaphore(name))

        ring = sb("ring", [P, RING, CH])
        wide = sb("wide", [P, KD, D])
        hres = sb("hres", [P, TT, D])
        xn = sb("xn", [P, TT, D])
        aT = sb("aT", [P, KD, T])
        junk = aT[:, :, :].rearrange("p k t -> p (k t)").rearrange("p (h n) -> p h n", h=TT)
        ident = sb("ident", [P, P])
        upper = sb("upper", [P, P])
        ones = sb("ones", [P, P])
        gcols = sb("gcols", [P, 3 * KD])
        wf = sb("wf", [P, KD, FOX_HEADS])
        wr = sb("wr", [P, KD, E])
        small = sb("small", [P, 224])
        col = [0]

        def cut(*shape):
            n = int(np.prod(shape))
            v = small[:, col[0]:col[0] + n]
            col[0] += n
            return v if len(shape) == 1 else v.rearrange("p (a b) -> p a b", a=shape[0])

        ssq, rstd, mhalf = cut(TT), cut(TT), cut(8)
        gains = cut(6)
        gq66, gk66, gq2, gk2, gsub, one = (gains[:, i:i + 1] for i in range(6))
        bf, z, zn, ze, logf = cut(8), cut(TT, 8), cut(TT, 8), cut(TT, 8), cut(TT, 8)
        cpos, cneg = cut(TT, 8), cut(TT, 8)
        ms, qr = cut(8), cut(8)
        lam, zlow = cut(6), cut(TT, 8)
        nmax, esum, rsum, nl = cut(2, 2), cut(2, 2), cut(2, 2), cut(2)
        dms, dr = cut(2), cut(2)

        arena = sb("arena", [P, 12576])

        def at(off, *shape):
            n = int(np.prod(shape))
            v = arena[:, off:off + n]
            if len(shape) == 2:
                v = v.rearrange("p (a b) -> p a b", a=shape[0])
            if len(shape) == 3:
                v = v.rearrange("p (a b c) -> p a b c", a=shape[0], b=shape[1])
            return v

        qkn = [at(0, 8, AUG), at(528, 8, AUG)]
        qkn_flat = [at(0, GROUP), at(528, GROUP)]
        fqT, fkT = at(1056, 8, T), at(3104, 8, T)
        vrow = at(1056, DIFF_HEADS, VROW)
        bucket = at(2592, VROW)
        relb = at(2976, DIFF_HEADS)
        lamv = at(2984, 4, HD)
        lamp = at(3240, 2, HD)
        grow = at(3368, P)
        dqT, dkT = at(5152, 4, T), at(6176, 4, T)
        fv, dv = at(7200, TT, GROUP), at(8224, TT, GROUP)
        t5 = at(9248, DIFF_HEADS, T)
        fmask = at(10272, T)
        S = [at(10528, VROW), at(10912, VROW)]
        PT = [at(11296, VROW), at(11680, VROW)]
        sq = at(12064, GROUP)

        b1r, b2r = at(1056, 2 * D), at(3104, D)
        pin, pT = at(3104, TT, 256), at(3616, TT, T)
        hT = at(0, 4, P)
        o = [4128]

        def take(*shape):
            v = at(o[0], *shape)
            o[0] += int(np.prod(shape))
            return v

        wp = take(TT, D)
        xsel = take(KD, 2 * SLOTS)
        glu, lin, sig, prod = take(512), take(512), take(512), take(512)
        outs = take(2, 512)
        Sel, SG, SGT = take(TT, 2 * SLOTS), take(TT, 3 * SLOTS), take(2, T)
        expert1 = take(2 * SLOTS)
        P1i, Gi = take(TT, COLS), take(TT, COLS)
        iota1, iotae, iota16, iotap = take(SLOTS), take(E), take(EXTRA), take(1)
        lg, mx8, idxf, e4, es = take(TT, E), take(TT, 8), take(TT, 8), take(TT, 4), take(TT)
        M, G, P1 = take(TT, E), take(TT, E), take(TT, E)
        oh, ohg = at(4128, TT, 4, E), at(4384, TT, 4, E)
        P1T, GT = at(0, T), at(256, T)
        cnt, extra, offs, over = at(512, 1), at(513, 1), at(514, MORE), at(518, MORE)
        Er, Eall, Bneg = at(522, MORE, EXTRA), at(570, COLS), at(620, COLS)
        nv0 = at(670, TT)
        brow = at(672, E)
        assert o[0] <= 12576, o[0]
        idx8 = sb("idx8", [P, TT, 8], U32)
        ints = sb("ints", [1, EXTRA + 1], I32)

        Y = [ctx.enter_context(nc.psum_tensor(f"sum{i}", [P, 512], F32)) for i in range(4)]
        H = ctx.enter_context(nc.psum_tensor("hidden", [P, 1024], F32))
        GB = ctx.enter_context(nc.psum_tensor("tokens", [P, 512], F32))
        TB = ctx.enter_context(nc.psum_tensor("outputs", [P, 512], F32))
        B = Y + [H[:, 0:512], H[:, 512:1024], GB, TB]
        skew = nc.dram_tensor("skew", (P, DIFF_HEADS * VROW), F32, kind="Internal").ap()

        names = """consts_made mhalf_made gain_ones gain_scaled masked_bucket vec_loaded head_loaded wf_loaded router_loaded
            gcols_T gcols_ready vrow_T vrow_ready skew_stored t5_loaded
            sums_ready mean_ready pow_done xn_ready xT_done xT_ready
            f_done z_ready fe_ready logf_ready cum_done c_ready lam_ready lam_exp
            proj_done sq_ready qk_scaled v_copied qk_ready turned turned_copied
            sc_done sc_masked sc_max exp_done comb_ready pt_done pt_copied pv_done pv_taken dsum_ready
            mixT_done mixT_copied wout_loaded out_done res_ready
            router_pe router_dve router_act tables_ready b_loaded b_used
            b1_cleared chunk_used sel_ready sg_ready expert_ready gath_done gath_taken glu_ready sig_ready
            hid_ready hT_done hT_taken out_taken sgt_done sgt_taken comb_done
            gate_loaded tail_loaded y_taken pT_done pT_ready pp_done gate_done sigmoid_ready gated y_final stored
            dve_turn act_turn pool_turn""".split()
        s = {n: sem(n) for n in names}
        x_loaded = [sem(f"x_loaded{i}") for i in range(TT)]
        win_loaded = [sem(f"win_loaded{i}") for i in range(RING)]
        chunk_loaded = [sem(f"chunk_loaded{i}") for i in range(RING)]

        w_in = a["w_in"][0]
        w1, w2 = a["w1"][0], a["w2"][0]

        def rows(ap):
            return ap.rearrange("(k p) n -> p k n", p=P)

        def unit_free(eng, u):
            if u in QK_UNITS:
                eng.wait_ge(s["qk_scaled"], QK_UNITS.index(u) + 1)
            else:
                eng.wait_ge(s["v_copied"], V_UNITS.index(u) + 1)

        turned_after, n_turned = {}, 0
        for step, i in ORDER:
            n_turned += {"qkT": 2 if i < 4 else 1, "pt": 1, "mix": 2}.get(step, 0)
            turned_after[step, i] = n_turned
        powers_before, n_powers = {}, TT
        for step, i in ORDER:
            if (step == "proj" and i in QK_UNITS) or (step == "pv" and i >= 8):
                powers_before[step, i] = n_powers
                n_powers += 1
        TRB = B[4:6]

        block = ctx.enter_context(nc.Block())

        @block.sync
        def _(sp):
            x, pe_in = a["x"][0], a["p"][0, 0]
            for tt in range(TT):
                sp.dma_start(hres[:, tt, :], x[tt * P:(tt + 1) * P, :]).then_inc(x_loaded[tt], 16)
            for c in range(RING):
                g, half = c // 2, c % 2
                src = rows(w_in[half * 512:(half + 1) * 512, GROUP_COL[g]:GROUP_COL[g] + GROUP])
                sp.dma_start(ring[:, c, :].rearrange("p (k n) -> p k n", k=4), src).then_inc(win_loaded[c], 16)
            sp.dma_start(wide[:, :, :], rows(a["w_out"][0])).then_inc(s["wout_loaded"], 16)

            def load_item(e, before):
                for c in range(RING):
                    before(c)
                    if c < KD:
                        sp.dma_start(ring[:, c, :], w1[e, c * P:(c + 1) * P, :]).then_inc(chunk_loaded[c], 16)
                    else:
                        j = c - KD
                        sp.dma_start(ring[:, c, :].rearrange("p (k n) -> p k n", k=2),
                                     rows(w2[e, 2 * j * P:2 * (j + 1) * P, :])).then_inc(chunk_loaded[c], 16)

            load_item(0, lambda c: sp.wait_ge(s["proj_done"], 2 * (c // 2) + 2))
            sp.wait_ge(s["pv_done"], 8)
            sp.wait_ge(s["sc_done"], 8)
            sp.wait_ge(s["b1_cleared"], 1)
            sp.dma_start(b1r[0:E, :], a["b1"][0]).then_inc(s["b_loaded"], 16)
            sp.dma_start(b2r[0:E, :], a["b2"][0]).then_inc(s["b_loaded"], 16)
            sp.wait_ge(s["out_done"], 4)
            sp.dma_start(wide[:, :, :], rows(a["w_ple_gate"][0])).then_inc(s["gate_loaded"], 16)
            sp.wait_ge(s["b_used"], 1)
            sp.dma_start(wp, rows(a["w_ple_proj"][0])).then_inc(s["tail_loaded"], 16)
            sp.dma_start(pin, pe_in.rearrange("(t p) n -> p t n", p=P)).then_inc(s["tail_loaded"], 16)
            with sp.Fori(1, E) as e:
                load_item(e, lambda c: sp.wait_ge(s["chunk_used"], (e - 1) * RING + (c + 1)))
            sp.wait_ge(s["tables_ready"], 1)
            n = sp.value_load(ints[0:1, EXTRA:EXTRA + 1], min_val=0, max_val=EXTRA)
            with sp.If(n > 0):
                with sp.Fori(0, (n + 1) // 2 * 2) as i:
                    e = sp.value_load(ints[0:1, bass.ds(i, 1)], min_val=0, max_val=E - 1)
                    load_item(e, lambda c: sp.wait_ge(s["chunk_used"], (i + (E - 1)) * RING + (c + 1)))
            for q in range(4):
                tt, half = q // 2, q % 2
                sp.wait_ge(s["y_final"], q + 1)
                sp.dma_start(out[0, tt * P:(tt + 1) * P, half * 512:(half + 1) * 512],
                             xn[:, tt, half * 512:(half + 1) * 512]).then_inc(s["stored"], 16)
            sp.wait_ge(s["stored"], 64)

        @block.gpsimd
        def _(pool):
            g = nc.gpsimd
            tn = Turns(pool, s["pool_turn"])
            g.memset(mhalf, -0.5).then_inc(s["mhalf_made"], 1)
            g.memset(ident[:, :], 0.0).then_inc(s["pool_turn"], 1)
            g.memset(ones[:, :], 1.0).then_inc(s["pool_turn"], 1)
            g.memset(fmask, 0.0).then_inc(s["pool_turn"], 1)
            tn.n = 3
            pool.wait_ge(s["pool_turn"], 3)
            g.affine_select(out=ident[:, :], in_=ident[:, :], compare_op=ALU.not_equal, fill=1.0, base=0,
                            pattern=[[-1, P]], channel_multiplier=1).then_inc(s["consts_made"], 1)
            g.affine_select(out=upper[:, :], in_=ones[:, :], compare_op=ALU.is_ge, fill=0.0, base=0,
                            pattern=[[1, P]], channel_multiplier=-1).then_inc(s["consts_made"], 1)
            g.affine_select(out=fmask[:, P:T], in_=fmask[:, P:T], compare_op=ALU.is_ge, fill=NEG, base=0,
                            pattern=[[-1, P]], channel_multiplier=1).then_inc(s["consts_made"], 1)
            pool.wait_ge(s["vrow_ready"], 1)
            pool.dma_start(skew[:, :].rearrange("p (h n) -> p h n", h=DIFF_HEADS),
                           vrow).then_inc(s["skew_stored"], 16)
            pows = {"norm": [(ssq[:, tt:tt + 1], rstd[:, tt:tt + 1]) for tt in range(TT)],
                    "qk": [(ms, qr)], "sub": [(dms, dr)]}
            k = 0

            def power(src, dst):
                nonlocal k
                k += 1
                pool.wait_ge(s["mean_ready"], k)
                g.tensor_tensor(dst, src, mhalf[:, 0:src.shape[1]], ALU.pow).then_inc(s["pow_done"], 1)

            for pair in pows["norm"]:
                power(*pair)
            pool.wait_ge(s["skew_stored"], 16)
            n = DIFF_HEADS * VROW
            back = bass.AP(skew.tensor, skew.offset + P - 1, [[n - 1, P], [VROW, DIFF_HEADS], [1, T]])
            pool.dma_start(t5, back).then_inc(s["t5_loaded"], 16)
            for step, i in ORDER:
                if step == "proj" and i in QK_UNITS:
                    power(*pows["qk"][0])
                if step == "pv" and i >= 8:
                    power(*pows["sub"][0])
            pool.wait_ge(s["sc_done"], 8)
            pool.wait_ge(s["pv_done"], 8)
            g.memset(b1r, 0.0).then_inc(s["b1_cleared"], 1)
            for pair in pows["norm"]:
                power(*pair)
            g.iota(iota1, [[1, SLOTS]], base=1, channel_multiplier=0,
                   allow_small_or_imprecise_dtypes=True).then_inc(s["consts_made"], 1)
            g.iota(iotae, [[1, E]], base=0, channel_multiplier=0,
                   allow_small_or_imprecise_dtypes=True).then_inc(s["consts_made"], 1)
            g.iota(iota16, [[1, EXTRA]], base=0, channel_multiplier=0,
                   allow_small_or_imprecise_dtypes=True).then_inc(s["consts_made"], 1)
            g.iota(iotap, [[0, 1]], base=0, channel_multiplier=1,
                   allow_small_or_imprecise_dtypes=True).then_inc(s["consts_made"], 1)
            for pair in pows["norm"]:
                power(*pair)

        @block.scalar
        def _(act):
            c = nc.scalar
            tn = Turns(act, s["act_turn"])
            for i, name in enumerate(("g_attn", "g_mlp", "g_ple")):
                act.dma_start(grow[i * KD:(i + 1) * KD, :],
                              a[name][0].rearrange("(k p) -> k p", p=P)).then_inc(s["vec_loaded"], 16)
            act.dma_start(relb[0:BUCKETS, :], a["rel_bias"]).then_inc(s["vec_loaded"], 16)
            act.dma_start(bucket[0:BUCKETS + 1, :], a["buckets"]).then_inc(s["vec_loaded"], 16)
            act.dma_start(wf[:, :, :], rows(w_in[:, FOX_F0:FOX_F0 + 8])).then_inc(s["wf_loaded"], 16)
            act.dma_start(bf, bass.AP(a["b_f"].tensor, a["b_f"].offset, [[0, P], [1, 8]])).then_inc(s["wf_loaded"], 16)
            act.wait_ge(s["gain_ones"], 1)
            for dst, name in ((gq66[0:HD], "g_fox_q"), (gk66[0:HD], "g_fox_k"), (gq2[0:HD], "g_diff_q"),
                              (gq2[HD:P], "g_diff_q"), (gk2[0:HD], "g_diff_k"), (gk2[HD:P], "g_diff_k"),
                              (gsub, "g_subln")):
                act.dma_start(dst, a[name].rearrange("a p -> p a")).then_inc(s["head_loaded"], 16)
            for i, name in enumerate(("lambda_q1", "lambda_k1", "lambda_q2", "lambda_k2")):
                act.dma_start(lamv[:, i, :], bass.AP(a[name].tensor, a[name].offset,
                                                     [[0, P], [1, HD]])).then_inc(s["head_loaded"], 16)
            act.dma_start(wr[:, :, :], rows(a["w_router"][0])).then_inc(s["router_loaded"], 16)
            act.wait_ge(s["vrow_T"], 1)
            for h in range(DIFF_HEADS):
                ins = c.copy(vrow[:, h, :], B[2 + h][:, 0:VROW])
            ins.then_inc(s["vrow_ready"], 1)

            def sums(first):
                for tt in range(TT):
                    first(tt)
                    c.activation(junk[:, tt, :], hres[:, tt, :], ACT.Square,
                                 accum_out=ssq[:, tt:tt + 1]).then_inc(s["sums_ready"], 1)

            sums(lambda tt: act.wait_ge(x_loaded[tt], 16))
            act.wait_ge(s["lam_ready"], 1)
            c.activation(lam[:, 2:4], lam[:, 0:2], ACT.Exp).then_inc(s["lam_exp"], 1)
            act.wait_ge(s["z_ready"], 1)
            tn.link(c.activation(ze, zn, ACT.Exp))
            c.activation(ze, ze, ACT.Ln, bias=one).then_inc(s["fe_ready"], 1)

            def tr_copy(j, dst, src, scale):
                act.wait_ge(s["turned"], j + 1)
                c.activation(dst, src, ACT.Copy if isinstance(scale, float) else ACT.Identity,
                             scale=scale).then_inc(s["turned_copied"], 1)

            act.wait_ge(s["head_loaded"], 16 * 11)
            act.wait_ge(s["gain_scaled"], 1)
            j = 0
            for step, i in ORDER:
                if step == "proj":
                    act.wait_ge(s["proj_done"], i + 1)
                    if i in QK_UNITS:
                        act.wait_ge(s["mean_ready"], powers_before[step, i])
                        c.activation(sq, B[i % 2][:, :], ACT.Square).then_inc(s["sq_ready"], 1)
                    else:
                        c.copy((fv if i < 6 else dv)[:, i % 2, :], B[i % 2][:, :]).then_inc(s["v_copied"], 1)
                elif step == "qkT":
                    tt = i % 2
                    if i < 4:
                        dst, gain = (fqT, gq66) if i < 2 else (fkT, gk66)
                        for b in range(2):
                            tr_copy(j, dst[0:AUG, 4 * b:4 * b + 4, tt * P:(tt + 1) * P],
                                    TRB[j % 2][0:AUG, :].rearrange("p (h t) -> p h t", h=4), gain[0:AUG])
                            j += 1
                    else:
                        dst, gain = (dqT, gq2) if i < 8 else (dkT, gk2)
                        tr_copy(j, dst[:, :, tt * P:(tt + 1) * P],
                                TRB[j % 2][:, :].rearrange("p (h t) -> p h t", h=4), gain)
                        j += 1
                elif step == "sc":
                    act.wait_ge(s["sc_max"], i + 1)
                    w = S[i % 2]
                    c.activation(w[:, 0:P], w[:, 0:P], ACT.Exp, bias=nmax[:, i % 2, 0:1],
                                 accum_out=esum[:, i % 2, 0:1]).then_inc(s["exp_done"], 1)
                    c.activation(w[:, P:VROW], w[:, P:VROW], ACT.Exp, bias=nmax[:, i % 2, 1:2],
                                 accum_out=esum[:, i % 2, 1:2]).then_inc(s["exp_done"], 1)
                elif step == "pt":
                    if i >= 2:
                        act.wait_ge(s["pv_done"], i - 1)
                    tr_copy(j, PT[i % 2], TRB[j % 2][:, 0:VROW], 1.0)
                    j += 1
                elif step == "pv" and i >= 8:
                    act.wait_ge(s["pv_done"], i + 1)
                    act.wait_ge(s["pow_done"], powers_before[step, i])
                    for b in range(TT):
                        ins = c.activation(sq[:, b * DV:(b + 1) * DV], B[6 + i % 2][:, b * DV:(b + 1) * DV],
                                           ACT.Square, accum_out=dms[:, b:b + 1])
                        ins.then_inc(s["dsum_ready"], 1)
                elif step == "mix":
                    for tt in range(TT):
                        tr_copy(j, aT[:, 4 * i:4 * i + 4, tt * P:(tt + 1) * P],
                                TRB[j % 2][:, :].rearrange("p (h t) -> p h t", h=4), gsub if i else 1.0)
                        j += 1
            act.dma_start(brow[0:1, :], a["b_router"]).then_inc(s["router_loaded"], 16)

            def after_out(tt):
                act.wait_ge(s["res_ready"], 2 * tt + 2)
                act.wait_ge(s["out_done"], 4)

            sums(after_out)
            act.wait_ge(s["router_dve"], 1)
            for tt in range(TT):
                c.activation(e4[:, tt, :], mx8[:, tt, 0:TOPK], ACT.Exp, bias=nv0[:, tt:tt + 1],
                             accum_out=es[:, tt:tt + 1]).then_inc(s["router_act"], 1)

            act.wait_ge(s["tables_ready"], 1)
            n = act.value_load(ints[0:1, EXTRA:EXTRA + 1], min_val=0, max_val=EXTRA)
            with act.Fori(0, (n + 1) // 2 + E // 2) as p:
                for i in range(2):
                    act.wait_ge(s["glu_ready"], 2 * p + (i + 1))
                    c.activation(sig, glu, ACT.Sigmoid, scale=ALPHA).then_inc(s["sig_ready"], 1)
                    if i == 0:
                        act.wait_ge(s["sgt_done"], p + 1)
                        c.copy(SGT.rearrange("p a t -> p (a t)"), GB[:, :]).then_inc(s["sgt_taken"], 1)
                    act.wait_ge(s["hT_done"], 2 * p + (i + 1))
                    c.copy(hT.rearrange("p k c -> p (k c)"), TB[:, :]).then_inc(s["hT_taken"], 1)
                    act.wait_ge(s["chunk_used"], 2 * RING * p + (i + 1) * RING)
                    c.copy(outs[0:SLOTS, i, :], TB[0:SLOTS, :])
                    c.copy(outs[SLOTS:P, 1 - i, :], TB[SLOTS:P, :]).then_inc(s["out_taken"], 1)

            def after_moe(tt):
                act.wait_ge(s["y_taken"], 2 * tt + 2)

            sums(after_moe)
            for q in range(4):
                act.wait_ge(s["gate_done"], q + 1)
                c.activation(ring[:, q, 0:512], Y[q][:, :], ACT.Sigmoid).then_inc(s["sigmoid_ready"], 1)

        @block.tensor
        def _(pe):
            mm, tr = nc.tensor.matmul, nc.tensor.transpose
            pe.wait_ge(s["consts_made"], 2)
            pe.wait_ge(s["vec_loaded"], 16 * 5)
            tr(B[0][:, 0:3 * KD], grow[0:3 * KD, :], ident[0:3 * KD, 0:3 * KD]).then_inc(s["gcols_T"], 1)
            pe.wait_ge(s["masked_bucket"], 1)
            for h in range(DIFF_HEADS):
                ins = mm(B[2 + h][:, 0:VROW], spread(relb[0:BUCKETS + 1, h], 1, P), bucket[0:BUCKETS + 1, :],
                         start=True, stop=True)
            ins.then_inc(s["vrow_T"], 1)

            def turn_x(k, banks, first):
                for tt in range(TT):
                    pe.wait_ge(s["xn_ready"], TT * k + tt + 1)
                    for b in range(2):
                        first(2 * tt + b)
                        for j in range(4):
                            ins = tr(banks[2 * tt + b][:, j * P:(j + 1) * P],
                                     xn[:, tt, (4 * b + j) * P:(4 * b + j + 1) * P], ident[:, :])
                        ins.then_inc(s["xT_done"], 1)

            turn_x(0, B[2:6], lambda q: pe.wait_ge(s["vrow_ready"], 1))
            pe.wait_ge(s["wf_loaded"], 32)
            for tt in range(TT):
                pe.wait_ge(s["xT_ready"], 2 * tt + 2)
                for k in range(KD):
                    ins = mm(B[6][:, 8 * tt:8 * tt + 8], aT[:, k, tt * P:(tt + 1) * P], wf[:, k, :],
                             start=(k == 0), stop=(k == KD - 1))
            ins.then_inc(s["f_done"], 1)

            j = 0

            def bank_turn():
                if j >= 2:
                    pe.wait_ge(s["turned_copied"], j - 1)
                return TRB[j % 2]

            for step, i in ORDER:
                if step == "proj":
                    g, tt = i // 2, i % 2
                    if i == 0:
                        pe.wait_ge(s["gcols_ready"], 1)
                    if i >= 2:
                        unit_free(pe, i - 2)
                    for k in range(KD):
                        if k % 4 == 0:
                            pe.wait_ge(win_loaded[2 * g + k // 4], 16)
                        ins = mm(B[i % 2][:, :], aT[:, k, tt * P:(tt + 1) * P],
                                 ring[:, 2 * g + k // 4, (k % 4) * GROUP:(k % 4 + 1) * GROUP],
                                 start=(k == 0), stop=(k == KD - 1))
                    ins.then_inc(s["proj_done"], 1)
                elif step == "cum":
                    pe.wait_ge(s["logf_ready"], 1)
                    mm(B[7][:, 0:8], upper[:, :], logf[:, 0, :], start=True, stop=True)
                    mm(B[7][:, 8:16], ones[:, :], logf[:, 0, :], start=True, stop=False)
                    mm(B[7][:, 8:16], upper[:, :], logf[:, 1, :], start=False, stop=True).then_inc(s["cum_done"], 1)
                elif step == "qkT":
                    pe.wait_ge(s["qk_ready" if i < 4 else "qk_scaled"], QK_UNITS.index(i) + 1)
                    if i < 4:
                        for b in range(2):
                            bank = bank_turn()
                            for h in range(4):
                                ins = tr(bank[0:AUG, h * P:(h + 1) * P], qkn[i % 2][:, 4 * b + h, :], ident[:, :])
                            ins.then_inc(s["turned"], 1)
                            j += 1
                    else:
                        bank = bank_turn()
                        for h in range(4):
                            ins = tr(bank[:, h * P:(h + 1) * P], qkn_flat[i % 2][:, h * P:(h + 1) * P], ident[:, :])
                        ins.then_inc(s["turned"], 1)
                        j += 1
                elif step == "sc":
                    bank = B[2 + i % 2]
                    if i == 0:
                        pe.wait_ge(s["turned_copied"], 8)
                    if i == 8:
                        pe.wait_ge(s["turned_copied"], turned_after["qkT", 9])
                    if i >= 2:
                        pe.wait_ge(s["sc_masked"], i - 1)
                    if i < 8:
                        q, k = fqT[0:AUG, i, :], fkT[0:AUG, i, :]
                    else:
                        h, m = (i - 8) // 2, i % 2
                        q, k = dqT[m * HD:(m + 1) * HD, h, :], dkT[m * HD:(m + 1) * HD, h, :]
                    mm(bank[:, 0:P], q[:, 0:P], k[:, 0:P], start=True, stop=True)
                    mm(bank[:, P:VROW], q[:, P:T], k[:, :], start=True, stop=True).then_inc(s["sc_done"], 1)
                elif step == "pt":
                    if i < 8:
                        pe.wait_ge(s["exp_done"], 2 * i + 2)
                    else:
                        pe.wait_ge(s["comb_ready"], i - 7)
                    bank, w = bank_turn(), S[i % 2 if i < 8 else 0]
                    for b in range(3):
                        ins = tr(bank[:, b * P:(b + 1) * P], w[:, b * P:(b + 1) * P], ident[:, :])
                    ins.then_inc(s["turned"], 1)
                    j += 1
                elif step == "pv":
                    bank, w = B[6 + i % 2], PT[i % 2]
                    pe.wait_ge(s["turned_copied"], turned_after["pt", i])
                    if i >= 2:
                        pe.wait_ge(s["pv_taken"], i - 1)
                    if i < 8:
                        v, n = [fv[:, t, i * HD:(i + 1) * HD] for t in range(TT)], HD
                    else:
                        v, n = [dv[:, t, (i - 8) * DV:(i - 7) * DV] for t in range(TT)], DV
                    if i in (0, 8):
                        pe.wait_ge(s["v_copied"], 2 if i < 8 else 4)
                    mm(bank[:, 0:n], w[:, 0:P], v[0], start=True, stop=True)
                    mm(bank[:, n:2 * n], w[:, P:T], v[0], start=True, stop=False)
                    mm(bank[:, n:2 * n], w[:, T:VROW], v[1], start=False, stop=True).then_inc(s["pv_done"], 1)
                elif step == "mix":
                    pe.wait_ge(s["pv_taken"], 12 if i else 8)
                    for tt in range(TT):
                        bank = bank_turn()
                        for b in range(4):
                            ins = tr(bank[:, b * P:(b + 1) * P], xn[:, tt, (4 * i + b) * P:(4 * i + b + 1) * P],
                                     ident[:, :])
                        ins.then_inc(s["turned"], 1)
                        j += 1
            pe.wait_ge(s["wout_loaded"], 16)
            pe.wait_ge(s["turned_copied"], j)
            for q, bank in enumerate((B[0], B[1], B[2], B[3])):
                tt, half = q // 2, q % 2
                for k in range(KD):
                    ins = mm(bank[:, :], aT[:, k, tt * P:(tt + 1) * P], wide[:, k, half * 512:(half + 1) * 512],
                             start=(k == 0), stop=(k == KD - 1))
                ins.then_inc(s["out_done"], 1)
            turn_x(1, B[4:8], lambda q: None)
            pe.wait_ge(s["router_loaded"], 32)
            pe.wait_ge(s["res_ready"], 4)
            for tt in range(TT):
                pe.wait_ge(s["xT_ready"], 4 + 2 * tt + 2)
                for k in range(KD):
                    mm(B[0][:, tt * E:(tt + 1) * E], aT[:, k, tt * P:(tt + 1) * P], wr[:, k, :],
                       start=(k == 0), stop=False)
                ins = mm(B[0][:, tt * E:(tt + 1) * E], ones[0:1, :], brow[0:1, :], start=False, stop=True)
            ins.then_inc(s["router_pe"], 1)
            pe.wait_ge(s["router_dve"], 2)
            mm(B[1][:, 0:E], upper[:, :], M[:, 0, :], start=True, stop=True)
            mm(B[1][:, E:2 * E], ones[:, :], M[:, 0, :], start=True, stop=False)
            mm(B[1][:, E:2 * E], upper[:, :], M[:, 1, :], start=False, stop=True)
            mm(B[1][0:E, 2 * E:2 * E + 1], M[:, 0, :], ones[:, 0:1], start=True, stop=False)
            mm(B[1][0:E, 2 * E:2 * E + 1], M[:, 1, :], ones[:, 0:1], start=False, stop=True) \
                .then_inc(s["router_pe"], 1)
            pe.wait_ge(s["router_dve"], 3)
            for q, src in enumerate((P1, G)):
                for tt in range(TT):
                    ins = tr(B[2][0:E, q * T + tt * P:q * T + (tt + 1) * P], src[:, tt, :], ident[:, :])
            ins.then_inc(s["router_pe"], 1)
            mm(B[3][0:E, 0:1], upper[0:E, 0:E], extra[0:E, :], start=True, stop=True)
            mm(B[3][0:1, 1:2], ones[0:E, 0:1], extra[0:E, :], start=True, stop=True).then_inc(s["router_pe"], 1)
            pe.wait_ge(s["router_dve"], 4)
            for tt in range(TT):
                mm(B[4][:, tt * COLS:(tt + 1) * COLS], P1T[0:E, tt * P:(tt + 1) * P], Eall[0:E, :],
                   start=True, stop=False)
                mm(B[4][:, tt * COLS:(tt + 1) * COLS], ones[0:E, :], Bneg[0:E, :], start=False, stop=True)
                mm(B[4][:, (TT + tt) * COLS:(TT + tt + 1) * COLS], GT[0:E, tt * P:(tt + 1) * P], Eall[0:E, :],
                   start=True, stop=True)
            mm(B[5][0:1, 0:EXTRA], iotap[0:E, :], Eall[0:E, E:ITEMS], start=True, stop=True) \
                .then_inc(s["router_pe"], 1)
            pe.wait_ge(s["b_loaded"], 32)
            for q in range(4):
                tt, half = q // 2, q % 2
                ins = mm(Y[q][:, :], GT[0:E, tt * P:(tt + 1) * P], b2r[0:E, half * 512:(half + 1) * 512],
                         start=True, stop=False, skip_group_check=True)
            ins.then_inc(s["b_used"], 1)

            def gather(b):
                for k in range(4):
                    for tt in range(TT):
                        ins = mm(GB[:, k * P:(k + 1) * P], xn[:, tt, (4 * b + k) * P:(4 * b + k + 1) * P],
                                 Sel[:, tt, :], start=(k == 0 and tt == 0), stop=(tt == 1), skip_group_check=True)
                ins.then_inc(s["gath_done"], 1)

            def combine():
                for q in range(4):
                    tt, half = q // 2, q % 2
                    ins = mm(Y[q][:, :], SGT[:, half, tt * P:(tt + 1) * P], outs[:, half, :],
                             start=False, stop=False, skip_group_check=True)
                ins.then_inc(s["comb_done"], 1)

            pe.wait_ge(s["tables_ready"], 1)
            pe.wait_ge(s["sel_ready"], 1)
            gather(0)
            pe.wait_ge(s["gath_taken"], 1)
            gather(1)
            n = pe.value_load(ints[0:1, EXTRA:EXTRA + 1], min_val=0, max_val=EXTRA)
            pairs = (n + 1) // 2 + E // 2
            with pe.Fori(0, pairs) as p:
                for i in range(2):
                    if i == 0:
                        pe.wait_ge(s["expert_ready"], p + 1)
                    for g in range(2):
                        for u in range(2):
                            c0 = u * D + g * 512
                            mm(H[u * SLOTS:(u + 1) * SLOTS, g * 512:(g + 1) * 512],
                               expert1[:, i * SLOTS:(i + 1) * SLOTS], b1r[:, c0:c0 + 512], start=True, stop=False)
                    for k in range(KD):
                        if i == 0 and k % 4 == 0:
                            pe.wait_ge(s["gath_taken"], 2 * p + (k // 4 + 1))
                        pe.wait_ge(chunk_loaded[k], (2 * p + (i + 1)) * 16)
                        for g in range(2):
                            for u in range(2):
                                c0 = u * D + g * 512
                                ins = mm(H[u * SLOTS:(u + 1) * SLOTS, g * 512:(g + 1) * 512],
                                         xsel[:, k, i * SLOTS:(i + 1) * SLOTS], ring[:, k, c0:c0 + 512],
                                         start=False, stop=(k == KD - 1))
                        ins.then_inc(s["chunk_used"], 1)
                    if i == 0:
                        pe.wait_ge(s["out_taken"], 2 * p + 2)
                        pe.wait_ge(s["sgt_taken"], p + 1)
                        combine()
                        pe.wait_ge(s["sg_ready"], p + 1)
                        for v in range(2):
                            for tt in range(TT):
                                ins = tr(GB[:, (2 * v + tt) * P:(2 * v + tt + 1) * P],
                                         SG[:, tt, v * SLOTS:v * SLOTS + P], ident[:, :])
                        ins.then_inc(s["sgt_done"], 1)
                    else:
                        pe.wait_ge(s["sel_ready"], p + 2)
                        pe.wait_ge(s["sgt_taken"], p + 2)
                        gather(0)
                    pe.wait_ge(s["hid_ready"], 2 * p + (i + 1))
                    if i:
                        pe.wait_ge(s["out_taken"], 2 * p + 3)
                    for k in range(4):
                        ins = tr(TB[:, k * P:(k + 1) * P], prod[:, k * P:(k + 1) * P], ident[:, :])
                    ins.then_inc(s["hT_done"], 1)
                    pe.wait_ge(s["hT_taken"], 2 * p + (i + 1))
                    for k in range(KD):
                        c = KD + k // 2
                        if k % 2 == 0:
                            pe.wait_ge(chunk_loaded[c], (2 * p + (i + 1)) * 16)
                        for u in range(2):
                            c0 = (k % 2) * D + (u ^ i) * 512
                            ins = mm(TB[u * SLOTS:(u + 1) * SLOTS, :],
                                     hT[:, k % 4, (k // 4) * SLOTS:(k // 4 + 1) * SLOTS], ring[:, c, c0:c0 + 512],
                                     start=(k == 0), stop=(k == KD - 1))
                        if k % 2:
                            ins.then_inc(s["chunk_used"], 1)
                    if i:
                        pe.wait_ge(s["gath_taken"], 2 * p + 3)
                        gather(1)
            pe.wait_ge(s["out_taken"], pairs * 2 + 2)
            pe.wait_ge(s["sgt_taken"], pairs + 1)
            combine()
            pe.wait_ge(s["tail_loaded"], 32)
            pe.wait_ge(s["gath_taken"], pairs * 2 + 2)
            for k in range(2):
                for tt in range(TT):
                    ins = tr(GB[:, k * T + tt * P:k * T + (tt + 1) * P], pin[:, tt, k * P:(k + 1) * P], ident[:, :])
            ins.then_inc(s["pT_done"], 1)
            pe.wait_ge(s["pT_ready"], 1)
            for q in range(4):
                tt, half = q // 2, q % 2
                for k in range(2):
                    ins = mm(B[4 + q][:, :], pT[:, k, tt * P:(tt + 1) * P], wp[:, k, half * 512:(half + 1) * 512],
                             start=(k == 0), stop=(k == 1))
            ins.then_inc(s["pp_done"], 1)
            turn_x(2, Y, lambda q: pe.wait_ge(s["y_taken"], q + 1))
            pe.wait_ge(s["gate_loaded"], 16)
            for q in range(4):
                tt, half = q // 2, q % 2
                pe.wait_ge(s["xT_ready"], 8 + max(q + 1, 2 * tt + 2))
                for k in range(KD):
                    ins = mm(Y[q][:, :], aT[:, k, tt * P:(tt + 1) * P], wide[:, k, half * 512:(half + 1) * 512],
                             start=(k == 0), stop=(k == KD - 1))
                ins.then_inc(s["gate_done"], 1)

        @block.vector
        def _(dve):
            v = nc.vector
            tn = Turns(dve, s["dve_turn"])
            v.memset(gains, 1.0).then_inc(s["gain_ones"], 1)
            v.memset(relb[BUCKETS:BUCKETS + 1, :], NEG).then_inc(s["masked_bucket"], 1)
            dve.wait_ge(s["gcols_T"], 1)
            v.tensor_copy(gcols[:, :], B[0][:, 0:3 * KD]).then_inc(s["gcols_ready"], 1)
            dve.wait_ge(s["gcols_ready"], 1)
            n_pow, n_x = 0, 0

            def request(ins):
                nonlocal n_pow
                n_pow += 1
                ins.then_inc(s["mean_ready"], 1)

            def mean(dst, src, n):
                request(v.tensor_scalar(dst, src, 1.0 / n, EPS, ALU.mult, ALU.add))

            def norm(k, banks, between):
                for tt in range(TT):
                    dve.wait_ge(s["sums_ready"], TT * k + tt + 1)
                    mean(ssq[:, tt:tt + 1], ssq[:, tt:tt + 1], D)
                first = n_pow - TT
                for tt in range(TT):
                    dve.wait_ge(s["pow_done"], first + tt + 1)
                    v.tensor_scalar(xn[:, tt, :], hres[:, tt, :], rstd[:, tt:tt + 1], None,
                                    ALU.mult).then_inc(s["xn_ready"], 1)
                between()
                for q in range(4):
                    tt, b = q // 2, q % 2
                    dve.wait_ge(s["xT_done"], 4 * k + q + 1)
                    v.tensor_tensor(aT[:, 4 * b:4 * b + 4, tt * P:(tt + 1) * P],
                                    banks[q][:, :].rearrange("p (k t) -> p k t", k=4),
                                    spread(gcols[:, KD * k + 4 * b:KD * k + 4 * b + 4], 2, P),
                                    ALU.mult).then_inc(s["xT_ready"], 1)

            def head_constants():
                dve.wait_ge(s["head_loaded"], 16 * 11)
                tn.link(v.tensor_tensor(lamp, lamv[:, 0:4:2, :], lamv[:, 1:4:2, :], ALU.mult))
                v.tensor_reduce(lam[:, 0:2], lamp, X, ALU.add).then_inc(s["lam_ready"], 1)
                v.tensor_scalar(gq66[0:HD], gq66[0:HD], HD ** -0.5, None, ALU.mult)
                v.tensor_scalar(gq2, gq2, HD ** -0.5, None, ALU.mult)
                v.tensor_scalar(gsub, gsub, 1.0 - LAM_INIT, None, ALU.mult).then_inc(s["gain_scaled"], 1)

            norm(0, B[2:6], head_constants)
            dve.wait_ge(s["lam_exp"], 1)
            tn.link(v.tensor_tensor(lam[:, 4:5], lam[:, 3:4], lam[:, 2:3], ALU.subtract))
            tn.link(v.tensor_scalar(lam[:, 5:6], lam[:, 4:5], -LAM_INIT, None, ALU.add))
            dve.wait_ge(s["f_done"], 1)
            dve.wait_ge(s["wf_loaded"], 32)
            tn.link(v.tensor_tensor(z, B[6][:, 0:16].rearrange("p (t h) -> p t h", t=TT), spread(bf, 1, TT),
                                    ALU.add))
            tn.link(v.tensor_scalar(zn, z, -1.0, None, ALU.mult))
            v.tensor_tensor(zn, z, zn, ALU.min).then_inc(s["z_ready"], 1)
            tn.link(v.tensor_scalar(zlow, z, 0.0, None, ALU.min))
            dve.wait_ge(s["fe_ready"], 1)
            v.tensor_tensor(logf, zlow, ze, ALU.subtract).then_inc(s["logf_ready"], 1)

            n_x = 0
            for step, i in ORDER:
                if step == "cum":
                    dve.wait_ge(s["cum_done"], 1)
                    c = B[7][:, 0:16].rearrange("p (t h) -> p t h", t=TT)
                    v.tensor_copy(cpos, c)
                    tn.link(v.tensor_scalar(cneg, c, -1.0, None, ALU.mult))
                elif step == "proj" and i in QK_UNITS:
                    u = QK_UNITS.index(i)
                    dve.wait_ge(s["sq_ready"], u + 1)
                    tn.link(v.tensor_reduce(ms, sq.rearrange("p (h d) -> p h d", h=8), X, ALU.add))
                    mean(ms, ms, HD)
                    dve.wait_ge(s["pow_done"], n_pow)
                    if i in (2, 3, 6, 7, 8, 9):
                        dve.wait_ge(s["turned"], turned_after["qkT", QK_UNITS[u - 2]])
                    dst = qkn[i % 2][:, :, 0:HD] if i < 4 else qkn_flat[i % 2].rearrange("p (h d) -> p h d", h=8)
                    v.tensor_tensor(dst, B[i % 2][:, :].rearrange("p (h d) -> p h d", h=8), spread(qr, 2, HD),
                                    ALU.mult).then_inc(s["qk_scaled"], 1)
                elif step == "qkT" and i < 4:
                    w, tt = qkn[i % 2], i % 2
                    gate, plain = (HD, HD + 1) if i < 2 else (HD + 1, HD)
                    v.tensor_copy(w[:, :, gate], (cpos if i < 2 else cneg)[:, tt, :])
                    v.memset(w[:, :, plain], 1.0).then_inc(s["qk_ready"], 1)
                elif step == "sc":
                    w, bank = S[i % 2], B[2 + i % 2]
                    dve.wait_ge(s["sc_done"], i + 1)
                    if 2 <= i < 10:
                        dve.wait_ge(s["turned"], turned_after["pt", i - 2])
                    elif i >= 10:
                        dve.wait_ge(s["turned"], turned_after["pt", i // 2 + 3])
                    if i == 0:
                        dve.wait_ge(s["consts_made"], 3)
                    if i == 8:
                        dve.wait_ge(s["t5_loaded"], 16)
                    bias = fmask if i < 8 else t5[:, (i - 8) // 2, :]
                    v.tensor_tensor(w[:, 0:P], bank[:, 0:P], bias[:, P:T], ALU.add)
                    v.tensor_tensor(w[:, P:VROW], bank[:, P:VROW], bias, ALU.add).then_inc(s["sc_masked"], 1)
                    dve.wait_ge(s["sc_masked"], i + 1)
                    v.tensor_reduce(nmax[:, i % 2, 0:1], w[:, 0:P], X, ALU.max, negate=True)
                    v.tensor_reduce(nmax[:, i % 2, 1:2], w[:, P:VROW], X, ALU.max,
                                    negate=True).then_inc(s["sc_max"], 1)
                elif step == "pt" and i < 8:
                    dve.wait_ge(s["exp_done"], 2 * i + 2)
                    tn.link(v.reciprocal(rsum[:, i % 2, :], esum[:, i % 2, :]))
                elif step == "pt":
                    dve.wait_ge(s["exp_done"], 4 * (i - 8) + 20)
                    tn.link(v.reciprocal(rsum, esum))
                    v.tensor_scalar(nl, rsum[:, 1, :], lam[:, 5:6], None, ALU.mult)
                    v.tensor_scalar(S[0][:, 0:P], S[0][:, 0:P], rsum[:, 0, 0:1], None, ALU.mult)
                    tn.link(v.tensor_scalar(S[0][:, P:VROW], S[0][:, P:VROW], rsum[:, 0, 1:2], None, ALU.mult))
                    v.scalar_tensor_tensor(out=S[0][:, 0:P], in0=S[1][:, 0:P], scalar=nl[:, 0:1],
                                           in1=S[0][:, 0:P], op0=ALU.mult, op1=ALU.add)
                    v.scalar_tensor_tensor(out=S[0][:, P:VROW], in0=S[1][:, P:VROW], scalar=nl[:, 1:2],
                                           in1=S[0][:, P:VROW], op0=ALU.mult,
                                           op1=ALU.add).then_inc(s["comb_ready"], 1)
                    dve.wait_ge(s["comb_ready"], i - 7)
                elif step == "pv":
                    bank, n = B[6 + i % 2], HD if i < 8 else DV
                    if i < 8:
                        dve.wait_ge(s["pv_done"], i + 1)
                        r, c0 = rsum[:, i % 2, :], i * HD
                    else:
                        dve.wait_ge(s["dsum_ready"], 2 * (i - 8) + 2)
                        mean(dms, dms, DV)
                        dve.wait_ge(s["pow_done"], n_pow)
                        r, c0 = dr, 512 + (i - 8) * DV
                    v.tensor_tensor(xn[:, :, c0:c0 + n], bank[:, 0:2 * n].rearrange("p (t d) -> p t d", t=TT),
                                    spread(r, 2, n), ALU.mult).then_inc(s["pv_taken"], 1)
                    dve.wait_ge(s["pv_taken"], i + 1)

            for q in range(4):
                tt, half = q // 2, q % 2
                dve.wait_ge(s["out_done"], q + 1)
                h = hres[:, tt, half * 512:(half + 1) * 512]
                v.tensor_tensor(h, B[q][:, :], h, ALU.add).then_inc(s["res_ready"], 1)
            norm(1, B[4:8], lambda: None)

            dve.wait_ge(s["router_pe"], 1)
            tn.link(v.tensor_copy(lg, B[0][:, 0:TT * E].rearrange("p (t e) -> p t e", t=TT)))
            for tt in range(TT):
                ins = v.max(mx8[:, tt, :], lg[:, tt, :])
            tn.link(ins)
            v.tensor_scalar(nv0, mx8[:, :, 0], -1.0, None, ALU.mult).then_inc(s["router_dve"], 1)
            for tt in range(TT):
                ins = v.max_index(idx8[:, tt, :], mx8[:, tt, :], lg[:, tt, :])
            tn.link(ins)
            tn.link(v.tensor_copy(idxf, idx8[:, :, :]))
            dve.wait_ge(s["consts_made"], 7)
            tn.link(v.tensor_tensor(oh, spread(spread(iotae, 1, TOPK), 1, TT), spread(idxf[:, :, 0:TOPK], 3, E),
                                    ALU.is_equal))
            v.tensor_reduce(M, oh.rearrange("p t j e -> p t e j"), X, ALU.add).then_inc(s["router_dve"], 1)
            dve.wait_ge(s["router_act"], TT)
            tn.link(v.reciprocal(es, es))
            tn.link(v.tensor_tensor(e4, e4, spread(es, 2, TOPK), ALU.mult))
            tn.link(v.tensor_tensor(ohg, oh, spread(e4, 3, E), ALU.mult))
            v.tensor_reduce(G, ohg.rearrange("p t j e -> p t e j"), X, ALU.add)
            dve.wait_ge(s["router_pe"], 2)
            dve.wait_ge(s["router_dve"], 2)
            v.tensor_tensor(P1, B[1][:, 0:TT * E].rearrange("p (t e) -> p t e", t=TT), M, ALU.mult)
            tn.link(v.tensor_copy(cnt[0:E], B[1][0:E, 2 * E:2 * E + 1]))
            for r in range(MORE):
                ins = v.tensor_scalar(over[0:E, r:r + 1], cnt[0:E], float(SLOTS * (r + 1)), None, ALU.is_gt)
            tn.link(ins)
            v.tensor_reduce(extra[0:E], over[0:E], X, ALU.add).then_inc(s["router_dve"], 1)
            v.memset(Eall, 0.0)
            tn.link(v.memset(Bneg[0:E], 0.0))
            v.tensor_copy(Eall[0:E, 0:E], ident[0:E, 0:E])
            dve.wait_ge(s["router_dve"], 3)
            dve.wait_ge(s["router_pe"], 4)
            v.tensor_copy(arena[0:E, 0:2 * T], B[2][0:E, :])
            v.tensor_copy(ints[0:1, EXTRA:EXTRA + 1], B[3][0:1, 1:2])
            tn.link(v.tensor_tensor(offs[0:E, 0:1], B[3][0:E, 0:1], extra[0:E], ALU.subtract))
            for r in range(1, MORE):
                ins = v.tensor_scalar(offs[0:E, r:r + 1], offs[0:E, 0:1], float(r), None, ALU.add)
            tn.link(ins)
            for r in range(MORE):
                ins = v.tensor_scalar(Er[0:E, r, :], iota16[0:E], offs[0:E, r:r + 1], over[0:E, r:r + 1],
                                      ALU.is_equal, ALU.mult)
            tn.link(ins)
            tail, base = Eall[0:E, E:ITEMS], Bneg[0:E, E:ITEMS]
            for r in range(MORE):
                tn.link(v.tensor_tensor(tail, tail, Er[0:E, r, :], ALU.add))
                ins = v.scalar_tensor_tensor(out=base, in0=Er[0:E, r, :], scalar=-float(SLOTS * (r + 1)), in1=base,
                                             op0=ALU.mult, op1=ALU.add)
                if r < MORE - 1:
                    tn.link(ins)
            ins.then_inc(s["router_dve"], 1)
            dve.wait_ge(s["router_pe"], 5)
            v.tensor_copy(P1i, B[4][:, 0:TT * COLS].rearrange("p (t i) -> p t i", t=TT))
            v.tensor_copy(Gi, B[4][:, TT * COLS:2 * TT * COLS].rearrange("p (t i) -> p t i", t=TT))
            v.tensor_copy(ints[0:1, 0:EXTRA], B[5][0:1, 0:EXTRA]).then_inc(s["tables_ready"], 1)
            dve.wait_ge(s["tables_ready"], 1)

            def of_pair(table, i):
                cols = table[:, :, bass.ds(i, 2)]
                return spread(cols, 3, SLOTS)

            def four(t, n):
                return t[:, :, 0:n * SLOTS].rearrange("p t (i c) -> p t i c", i=n)

            def select(i):
                v.tensor_tensor(four(Sel, 2), spread(spread(iota1, 1, 2), 1, TT), of_pair(P1i, i),
                                ALU.is_equal).then_inc(s["sel_ready"], 1)

            def weigh(i):
                v.tensor_tensor(four(SG, 2), four(Sel, 2), of_pair(Gi, i), ALU.mult)
                v.tensor_tensor(SG[:, :, 2 * SLOTS:], Sel[:, :, 0:SLOTS],
                                spread(Gi[:, :, bass.ds(i, 1)][:, :, 0], 2, SLOTS), ALU.mult).then_inc(s["sg_ready"], 1)

            def bias_of(i):
                v.tensor_copy(expert1.rearrange("p (i c) -> p i c", i=2),
                              spread(Eall[:, bass.ds(i, 2)], 2, SLOTS)).then_inc(s["expert_ready"], 1)

            def take_tokens(b):
                v.tensor_tensor(xsel[:, 4 * b:4 * b + 4, :], GB[:, :].rearrange("p (k c) -> p k c", k=4),
                                spread(gcols[:, KD + 4 * b:KD + 4 * b + 4], 2, P),
                                ALU.mult).then_inc(s["gath_taken"], 1)

            v.memset(outs, 0.0).then_inc(s["out_taken"], 2)
            v.memset(SGT, 0.0).then_inc(s["sgt_taken"], 1)
            select(0)
            dve.wait_ge(s["sel_ready"], 1)
            weigh(0)
            bias_of(0)
            for b in range(2):
                dve.wait_ge(s["gath_done"], b + 1)
                take_tokens(b)
            n = dve.value_load(ints[0:1, EXTRA:EXTRA + 1], min_val=0, max_val=EXTRA)
            pairs = (n + 1) // 2 + E // 2
            before, per = tn.n, 4
            with dve.Fori(0, pairs) as p:
                tn.base, tn.n = p * per + before, 0
                for i in range(2):
                    dve.wait_ge(s["chunk_used"], 2 * RING * p + (i * RING + KD))
                    v.tensor_scalar(glu, H[:, 0:1024:2], LIMIT, None, ALU.min).then_inc(s["glu_ready"], 1)
                    tn.link(v.tensor_scalar(lin, H[:, 1:1024:2], -LIMIT, LIMIT, ALU.max, ALU.min))
                    tn.link(v.scalar_tensor_tensor(out=lin, in0=lin, scalar=1.0, in1=glu, op0=ALU.add,
                                                   op1=ALU.mult))
                    dve.wait_ge(s["sig_ready"], 2 * p + (i + 1))
                    v.tensor_tensor(prod, lin, sig, ALU.mult).then_inc(s["hid_ready"], 1)
                    if i == 0:
                        select(2 * p + 2)
                        dve.wait_ge(s["sel_ready"], p + 2)
                        dve.wait_ge(s["sgt_done"], p + 1)
                        weigh(2 * p + 2)
                    else:
                        bias_of(2 * p + 2)
                        for b in range(2):
                            dve.wait_ge(s["gath_done"], 2 * p + (b + 3))
                            take_tokens(b)
                assert tn.n == per

            dve.wait_ge(s["comb_done"], pairs + 1)
            for q in range(4):
                tt, half = q // 2, q % 2
                h = hres[:, tt, half * 512:(half + 1) * 512]
                v.tensor_tensor(h, Y[q][:, :], h, ALU.add).then_inc(s["y_taken"], 1)

            def embedding():
                dve.wait_ge(s["pT_done"], 1)
                v.tensor_copy(pT, GB[:, :].rearrange("p (k t) -> p k t", k=2)).then_inc(s["pT_ready"], 1)

            embedding()
            norm(2, Y, lambda: None)
            dve.wait_ge(s["pp_done"], 1)
            for q in range(4):
                tt, half = q // 2, q % 2
                g = ring[:, q, 0:512]
                dve.wait_ge(s["sigmoid_ready"], q + 1)
                v.tensor_tensor(g, B[4 + q][:, :], g, ALU.mult).then_inc(s["gated"], 1)
                dve.wait_ge(s["gated"], q + 1)
                v.tensor_tensor(xn[:, tt, half * 512:(half + 1) * 512], g,
                                hres[:, tt, half * 512:(half + 1) * 512], ALU.add).then_inc(s["y_final"], 1)


INPUTS = ["x", "p", "rel_bias", "g_attn", "w_in", "b_f", "g_fox_q", "g_fox_k", "g_diff_q", "g_diff_k",
          "lambda_q1", "lambda_k1", "lambda_q2", "lambda_k2", "g_subln", "w_out", "g_mlp", "w_router", "b_router",
          "w1", "b1", "w2", "b2", "g_ple", "w_ple_gate", "w_ple_proj"]


def bucket_table():
    table = np.zeros((BUCKETS + 1, VROW), np.float32)
    exact = BUCKETS // 2
    for n in range(VROW):
        rel = 2 * P - 1 - n
        if rel < 0:
            bucket = BUCKETS
        elif rel < exact:
            bucket = rel
        else:
            bucket = min(BUCKETS - 1, exact + int(np.log(rel / exact) / np.log(P / exact) * (BUCKETS - exact) + 1e-9))
        table[bucket, n] = 1.0
    return table


def kernel(**inputs):
    import concourse.bacc as bacc
    from concourse.bass_utils import run_bass_kernel_spmd as run

    nc = bacc.Bacc("TRN2", target_bir_lowering=False, num_devices=1)
    arrays, args = {}, {}
    named = {name: np.asarray(inputs[name]) for name in INPUTS}
    named["buckets"] = bucket_table()
    for name, v in named.items():
        arrays[f"in_{name}"] = v
        args[name] = nc.dram_tensor(f"in_{name}", v.shape, mybir.dt.from_np(v.dtype), kind="ExternalInput").ap()
    out = nc.dram_tensor("out_dram", (1, T, D), F32, kind="ExternalOutput").ap()
    build(nc, args, out)
    return run(nc, [arrays], core_ids=[0]).results[0]["out_dram"]
```

```python
import numpy as np
import concourse.bass as bass
from concourse import mybir
from concourse.alu_op_type import AluOpType as ALU
from contextlib import ExitStack

F32 = mybir.dt.float32
I32 = mybir.dt.int32
U32 = mybir.dt.uint32
ACT = mybir.ActivationFunctionType
X = mybir.AxisListType.X

P = 128
T = 256
TT = T // P
D = 1024
KD = D // P
FOX_HEADS, DIFF_HEADS, HD, DV = 8, 4, 64, 128
AUG = HD + 2
FOX_F0 = 3 * FOX_HEADS * HD
GROUP = 512
GROUP_COL = [0, 512, 1024, FOX_F0 + 8, FOX_F0 + 520, FOX_F0 + 1032]
UNITS = 12
QK_UNITS = [0, 1, 2, 3, 6, 7, 8, 9]
V_UNITS = [4, 5, 10, 11]
EPS = 1e-6
NEG = -1e30
LAM_INIT = 0.8 - 0.6 * 1.0
ALPHA, LIMIT = 1.702, 7.0
BUCKETS, VROW = 32, 384

E = 32
TOPK = 4
SLOTS = 64
MORE = T // SLOTS - 1
EXTRA = T * TOPK // SLOTS
ITEMS = E + EXTRA
COLS = ITEMS + 2
RING = 12
CH = 2048
PLE_PAIR = 8
PARTS = [(0, 0, 512), (0, 512, 512), (1, 0, 512), (1, 512, 256), (1, 768, 256)]
EARLY = 5

ORDER = ([("proj", 0), ("cum", 0)]
         + [s for u in range(1, 5) for s in (("proj", u), ("qkT", u - 1))]
         + [("proj", 5), ("sc", 0), ("sc", 1)]
         + [("proj", 6), ("pt", 0), ("pt", 1), ("sc", 2), ("sc", 3)]
         + [("proj", 7), ("qkT", 6), ("pv", 0), ("pv", 1), ("pt", 2), ("pt", 3), ("sc", 4), ("sc", 5)]
         + [("proj", 8), ("qkT", 7), ("pv", 2), ("pv", 3), ("pt", 4), ("pt", 5), ("sc", 6), ("sc", 7)]
         + [("proj", 9), ("qkT", 8), ("pv", 4), ("pv", 5), ("pt", 6), ("pt", 7)]
         + [("proj", 10), ("qkT", 9), ("pv", 6), ("pv", 7), ("sc", 8), ("sc", 9)]
         + [("proj", 11), ("pt", 8), ("mix", 0), ("sc", 10), ("sc", 11), ("out", 0)]
         + [("sc", 12), ("sc", 13), ("out", 1), ("pt", 9)]
         + [("sc", 14), ("sc", 15), ("pv", 8), ("out", 2), ("pt", 10), ("pt", 11)]
         + [("pv", 9), ("pv", 10), ("pv", 11), ("out", 3), ("mix", 1)])


def spread(ap, axis, n):
    dims = [list(d) for d in ap.ap]
    dims.insert(axis, [0, n])
    return bass.AP(ap.tensor, ap.offset, dims)


class Turns:

    def __init__(self, eng, sem):
        self.eng, self.sem, self.n, self.base = eng, sem, 0, 0

    def step(self, ins):
        ins.then_inc(self.sem, 1)
        self.n += 1

    def link(self, ins):
        self.step(ins)
        self.eng.wait_ge(self.sem, self.base + self.n)


def build(nc, a, out):
    with ExitStack() as ctx:
        def sb(name, shape, dt=F32):
            return ctx.enter_context(nc.sbuf_tensor(name, shape, dt))

        def sem(name):
            return ctx.enter_context(nc.semaphore(name))

        ring = sb("ring", [P, RING, CH])
        wide = sb("wide", [P, KD, D])
        hres = sb("hres", [P, TT, D])
        xn = sb("xn", [P, TT, D])
        aT = sb("aT", [P, KD, T])
        junk = aT[:, :, :].rearrange("p k t -> p (k t)").rearrange("p (h n) -> p h n", h=TT)
        ident = sb("ident", [P, P])
        upper = sb("upper", [P, P])
        ones = sb("ones", [P, P])
        gcols = sb("gcols", [P, 3 * KD])
        wf = sb("wf", [P, KD, FOX_HEADS])
        wr = sb("wr", [P, KD, E])
        small = sb("small", [P, 246])
        col = [0]

        def cut(*shape):
            n = int(np.prod(shape))
            v = small[:, col[0]:col[0] + n]
            col[0] += n
            return v if len(shape) == 1 else v.rearrange("p (a b) -> p a b", a=shape[0])

        ssq, rstd, mhalf = cut(TT), cut(TT), cut(8)
        gains = cut(6)
        gq66, gk66, gq2, gk2, gsub, one = (gains[:, i:i + 1] for i in range(6))
        bf, z, zn, ze, logf = cut(8), cut(TT, 8), cut(TT, 8), cut(TT, 8), cut(TT, 8)
        cpos, cneg = cut(TT, 8), cut(TT, 8)
        ms, qr = cut(8), cut(8)
        lam, zlow = cut(6), cut(TT, 8)
        nmax, esum, rsum, nl = cut(4, 2), cut(4, 2), cut(8, 2), cut(2)
        dms, dr, dr2 = cut(2), cut(2), cut(2)

        arena = sb("arena", [P, 12576])

        def at(off, *shape):
            n = int(np.prod(shape))
            v = arena[:, off:off + n]
            if len(shape) == 2:
                v = v.rearrange("p (a b) -> p a b", a=shape[0])
            if len(shape) == 3:
                v = v.rearrange("p (a b c) -> p a b c", a=shape[0], b=shape[1])
            return v

        qkn = [at(0, 8, AUG), at(528, 8, AUG)]
        qkn_flat = [at(0, GROUP), at(528, GROUP)]
        fqT, fkT = at(1056, 8, T), at(3104, 8, T)
        vrow = at(10528, VROW)
        bucket = at(2592, VROW)
        relb = at(2976, DIFF_HEADS)
        lamv = at(2984, 4, HD)
        lamp = at(3240, 2, HD)
        grow = at(3368, P)
        fT = at(3496, T)
        dqT, dkT = at(5152, 4, T), at(6176, 4, T)
        fv, dv = at(7200, TT, GROUP), at(8224, TT, GROUP)
        t5 = at(9248, DIFF_HEADS, T)
        fmask = at(10272, T)
        S = [at(10528, VROW), at(10912, VROW), at(0, VROW), at(VROW, VROW)]
        PT = [at(11296, VROW), at(11680, VROW)]
        sq = at(12064, GROUP)

        b1r, b2r = at(1056, 2 * D), at(3104, D)
        pin, pT = at(3104, TT, 256), at(3616, TT, T)
        hT = at(0, 4, P)
        o = [4128]

        def take(*shape):
            v = at(o[0], *shape)
            o[0] += int(np.prod(shape))
            return v

        wp = take(TT, D)
        xsel = take(KD, 2 * SLOTS)
        glu, lin, sig, prod = take(512), take(512), take(512), take(512)
        outs = take(2, 512)
        Sel, SG, SGT = take(TT, 2 * SLOTS), take(TT, 3 * SLOTS), take(2, T)
        expert1 = take(2 * SLOTS)
        P1i, Gi = take(TT, COLS), take(TT, COLS)
        iota1, iotae, iota16, iotap = take(SLOTS), take(E), take(EXTRA), take(1)
        lg, mx8, idxf, e4, es = take(TT, E), take(TT, 8), take(TT, 8), take(TT, 4), take(TT)
        M = take(TT, E)
        oh, ohg = at(4128, TT, 4, E), at(4384, TT, 4, E)
        P1T, GT = at(0, T), at(256, T)
        cnt, extra, offs, over = at(512, 1), at(513, 1), at(514, MORE), at(518, MORE)
        Er, Eall, Bneg = at(522, MORE, EXTRA), at(570, COLS), at(620, EXTRA + 2)
        nv0 = at(670, TT)
        mid_junk = at(5152, TT, D)
        bcol = at(672, 1)
        lT = at(712, T)
        halfsum = dms
        assert o[0] <= 12576, o[0]
        idx8 = sb("idx8", [P, TT, 8], U32)
        ints = sb("ints", [1, EXTRA + 1], I32)

        Y = [ctx.enter_context(nc.psum_tensor(f"sum{i}", [P, 512], F32)) for i in range(4)]
        H = ctx.enter_context(nc.psum_tensor("hidden", [P, 1024], F32))
        GB = ctx.enter_context(nc.psum_tensor("tokens", [P, 512], F32))
        TB = ctx.enter_context(nc.psum_tensor("outputs", [P, 512], F32))
        B = Y + [H[:, 0:512], H[:, 512:1024], GB, TB]
        skew = nc.dram_tensor("skew", (P, DIFF_HEADS * VROW), F32, kind="Internal").ap()

        names = """consts_made mhalf_made gain_ones gain_scaled masked_bucket vec_loaded head_loaded wf_loaded router_loaded
            gcols_T gcols_ready vrow_T vrow_ready skew_stored t5_loaded
            sums_ready mean_ready pow_done xn_ready xT_done xT_ready
            fT_done fT_copied f_done z_ready fe_ready logf_ready cum_done c_ready lam_ready lam_exp
            proj_done sq_ready qk_scaled v_copied qk_ready turned turned_copied
            sc_done sc_masked sc_max exp_done comb_ready pt_done pt_copied pv_done pv_taken dsum_ready
            mixT_done mixT_copied wout_loaded out_done res_ready
            logitsT_done lT_ready logits_done top_ready mask_ready gate_exp ranks_done ranks_taken extra_ready byexpert_T byexpert_ready offs_done
            items_ready tables_done tables_ready iotas_made b_loaded b_used
            b1_cleared gt_cleared chunk_used sel_ready sg_ready expert_ready gath_done gath_taken glu_ready sig_ready
            hid_ready hT_done hT_taken out_taken sgt_done sgt_taken y_done
            gate_loaded tail_loaded y_taken pT_done pT_ready pp_done pp_taken ple_ready gate_done sigmoid_ready gated y_final stored
            dve_turn act_turn pool_turn""".split()
        s = {n: sem(n) for n in names}
        x_loaded = [sem(f"x_loaded{i}") for i in range(TT)]
        win_loaded = [sem(f"win_loaded{i}") for i in range(RING)]
        chunk_loaded = [sem(f"chunk_loaded{i}") for i in range(RING)]

        w_in = a["w_in"][0]
        w1, w2 = a["w1"][0], a["w2"][0]

        def rows(ap):
            return ap.rearrange("(k p) n -> p k n", p=P)

        def unit_free(eng, u):
            if u in QK_UNITS:
                eng.wait_ge(s["qk_scaled"], QK_UNITS.index(u) + 1)
            else:
                eng.wait_ge(s["v_copied"], V_UNITS.index(u) + 1)

        turned_after, n_turned = {}, 0
        for step, i in ORDER:
            n_turned += {"qkT": 2 if i < 4 else 1, "pt": 1, "mix": 2}.get(step, 0)
            turned_after[step, i] = n_turned
        powers_before, n_powers = {}, TT
        for step, i in ORDER:
            if (step == "proj" and i in QK_UNITS) or (step == "pv" and i >= 8):
                powers_before[step, i] = n_powers
                n_powers += 1

        def buf(i):
            return i % 2 if i < 8 else i % 4

        def first_buf(job):
            return job % 2 if job < 8 else 2 * (job % 2)

        def first_sum(job):
            return job % 2 if job < 8 else 2 * (job - 8)

        TRB = B[4:6]

        def gate_bank(tt, c0, n):
            bank = Y[0] if (tt, c0, n) == PARTS[-1] else B[4 + 2 * tt + c0 // 512]
            return bank[:, 0:n]

        early = [wide[:, 2 * c:2 * c + 2, :].rearrange("p k n -> p (k n)") for c in range(4)]
        early.append(aT[:, :, :].rearrange("p k t -> p (k t)"))

        block = ctx.enter_context(nc.Block())

        @block.sync
        def _(sp):
            x, pe_in = a["x"][0], a["p"][0, 0]
            for tt in range(TT):
                sp.dma_start(hres[:, tt, :], x[tt * P:(tt + 1) * P, :]).then_inc(x_loaded[tt], 16)
            for c in range(RING):
                g, half = c // 2, c % 2
                if c == 0:
                    sp.wait_ge(s["vec_loaded"], 16 * 5)
                if c == 2:
                    sp.wait_ge(s["wf_loaded"], 16 * 2)
                    sp.wait_ge(s["head_loaded"], 16 * 11)
                src = rows(w_in[half * 512:(half + 1) * 512, GROUP_COL[g]:GROUP_COL[g] + GROUP])
                sp.dma_start(ring[:, c, :].rearrange("p (k n) -> p k n", k=4), src).then_inc(win_loaded[c], 16)
            sp.dma_start(wide[:, :, :], rows(a["w_out"][0])).then_inc(s["wout_loaded"], 16)

            def load(e, c, dst):
                if c < KD:
                    sp.dma_start(dst, w1[e, c * P:(c + 1) * P, :]).then_inc(chunk_loaded[c], 16)
                else:
                    j = c - KD
                    sp.dma_start(dst.rearrange("p (k n) -> p k n", k=2),
                                 rows(w2[e, 2 * j * P:2 * (j + 1) * P, :])).then_inc(chunk_loaded[c], 16)

            def load_item(e, before, chunks=range(RING)):
                for c in chunks:
                    before(c)
                    load(e, c, ring[:, c, :])

            load_item(0, lambda c: sp.wait_ge(s["proj_done"], 2 * (c // 2) + 2))
            sp.wait_ge(s["pv_done"], 8)
            sp.wait_ge(s["sc_done"], 8)
            sp.wait_ge(s["b1_cleared"], 1)
            sp.dma_start(b1r[0:E, :], a["b1"][0]).then_inc(s["b_loaded"], 16)
            sp.dma_start(b2r[0:E, :], a["b2"][0]).then_inc(s["b_loaded"], 16)
            sp.wait_ge(s["out_done"], 4)
            for c in range(4):
                load(1, c, early[c])
            sp.wait_ge(s["logitsT_done"], TT)
            load(1, 4, early[4])
            sp.wait_ge(s["b_used"], 1)
            sp.dma_start(wp, rows(a["w_ple_proj"][0])).then_inc(s["tail_loaded"], 16)
            sp.dma_start(pin, pe_in.rearrange("(t p) n -> p t n", p=P)).then_inc(s["tail_loaded"], 16)
            for c in range(EARLY):
                sp.wait_ge(chunk_loaded[c], 32)
                sp.wait_ge(s["chunk_used"], c + 1)
                load(2, c, ring[:, c, :])
            load_item(1, lambda c: sp.wait_ge(s["chunk_used"], c + 1), range(EARLY, RING))
            load_item(2, lambda c: sp.wait_ge(s["chunk_used"], RING + c + 1), range(EARLY, RING))
            with sp.Fori(3, E) as e:
                load_item(e, lambda c: sp.wait_ge(s["chunk_used"], (e - 1) * RING + (c + 1)))
            sp.wait_ge(s["tables_ready"], 1)
            n = sp.value_load(ints[0:1, EXTRA:EXTRA + 1], min_val=0, max_val=EXTRA)
            with sp.If(n > 0):
                with sp.Fori(0, (n + 1) // 2 * 2) as i:
                    e = sp.value_load(ints[0:1, bass.ds(i, 1)], min_val=0, max_val=E - 1)
                    load_item(e, lambda c: sp.wait_ge(s["chunk_used"], (i + (E - 1)) * RING + (c + 1)))
            sp.wait_ge(s["chunk_used"], RING + EARLY)
            sp.dma_start(wide[:, :, :], rows(a["w_ple_gate"][0])).then_inc(s["gate_loaded"], 16)
            for q, (tt, c0, n) in enumerate(PARTS):
                sp.wait_ge(s["y_final"], q + 1)
                sp.dma_start(out[0, tt * P:(tt + 1) * P, c0:c0 + n], xn[:, tt, c0:c0 + n]).then_inc(s["stored"], 16)
            sp.wait_ge(s["stored"], 16 * len(PARTS))

        @block.gpsimd
        def _(pool):
            g = nc.gpsimd
            tn = Turns(pool, s["pool_turn"])
            g.memset(mhalf, -0.5).then_inc(s["mhalf_made"], 1)
            g.memset(ident[:, :], 0.0).then_inc(s["pool_turn"], 1)
            g.memset(ones[:, :], 1.0).then_inc(s["pool_turn"], 1)
            g.memset(fmask, 0.0).then_inc(s["pool_turn"], 1)
            tn.n = 3
            pool.wait_ge(s["pool_turn"], 3)
            g.affine_select(out=ident[:, :], in_=ident[:, :], compare_op=ALU.not_equal, fill=1.0, base=0,
                            pattern=[[-1, P]], channel_multiplier=1).then_inc(s["consts_made"], 1)
            g.affine_select(out=upper[:, :], in_=ones[:, :], compare_op=ALU.is_ge, fill=0.0, base=0,
                            pattern=[[1, P]], channel_multiplier=-1).then_inc(s["consts_made"], 1)
            g.affine_select(out=fmask[:, P:T], in_=fmask[:, P:T], compare_op=ALU.is_ge, fill=NEG, base=0,
                            pattern=[[-1, P]], channel_multiplier=1).then_inc(s["consts_made"], 1)
            pows = {"norm": [(ssq[:, tt:tt + 1], rstd[:, tt:tt + 1]) for tt in range(TT)],
                    "qk": [(ms, qr)], "sub": [(dms, dr)]}
            k = 0

            def power(src, dst):
                nonlocal k
                k += 1
                pool.wait_ge(s["mean_ready"], k)
                g.tensor_tensor(dst, src, mhalf[:, 0:src.shape[1]], ALU.pow).then_inc(s["pow_done"], 1)

            for pair in pows["norm"]:
                power(*pair)
            pool.wait_ge(s["vrow_ready"], 1)
            pool.dma_start(skew[:, :].rearrange("p (h n) -> h p n", h=DIFF_HEADS),
                           spread(vrow[0:DIFF_HEADS, :], 1, P)).then_inc(s["skew_stored"], 16)
            n = DIFF_HEADS * VROW
            back = bass.AP(skew.tensor, skew.offset + P - 1, [[n - 1, P], [VROW, DIFF_HEADS], [1, T]])
            for step, i in ORDER:
                if (step, i) == ("proj", 6):
                    pool.wait_ge(s["skew_stored"], 16)
                    pool.dma_start(t5, back).then_inc(s["t5_loaded"], 16)
                if step == "proj" and i in QK_UNITS:
                    power(*pows["qk"][0])
                if step == "pv" and i >= 8:
                    power(*pows["sub"][0])
            pool.wait_ge(s["pv_done"], 12)
            pool.wait_ge(s["sc_masked"], 16)
            g.iota(iota1, [[1, SLOTS]], base=1, channel_multiplier=0,
                   allow_small_or_imprecise_dtypes=True).then_inc(s["iotas_made"], 1)
            g.iota(iotae, [[1, E]], base=0, channel_multiplier=0,
                   allow_small_or_imprecise_dtypes=True).then_inc(s["iotas_made"], 1)
            g.iota(iota16, [[1, EXTRA]], base=0, channel_multiplier=0,
                   allow_small_or_imprecise_dtypes=True).then_inc(s["iotas_made"], 1)
            g.iota(iotap, [[0, 1]], base=0, channel_multiplier=1,
                   allow_small_or_imprecise_dtypes=True).then_inc(s["iotas_made"], 1)
            g.memset(arena[:, 1056:4128], 0.0).then_inc(s["b1_cleared"], 1)
            g.memset(GT, 0.0).then_inc(s["gt_cleared"], 1)
            g.memset(outs, 0.0).then_inc(s["out_taken"], 2)
            g.memset(SGT, 0.0).then_inc(s["sgt_taken"], 1)
            for pair in pows["norm"]:
                power(*pair)
            for pair in pows["norm"]:
                power(*pair)

        @block.scalar
        def _(act):
            c = nc.scalar
            tn = Turns(act, s["act_turn"])
            act.dma_start(bucket[0:BUCKETS + 1, :], a["buckets"]).then_inc(s["vec_loaded"], 16)
            act.dma_start(relb[0:BUCKETS, :], a["rel_bias"]).then_inc(s["vec_loaded"], 16)
            for i, name in enumerate(("g_attn", "g_mlp", "g_ple")):
                act.dma_start(grow[i * KD:(i + 1) * KD, :],
                              a[name][0].rearrange("(k p) -> k p", p=P)).then_inc(s["vec_loaded"], 16)
            act.dma_start(wf[:, :, :], rows(w_in[:, FOX_F0:FOX_F0 + 8])).then_inc(s["wf_loaded"], 16)
            act.dma_start(bf, bass.AP(a["b_f"].tensor, a["b_f"].offset, [[0, P], [1, 8]])).then_inc(s["wf_loaded"], 16)

            def sums(tt, scratch):
                c.activation(scratch[:, tt, :], hres[:, tt, :], ACT.Square,
                             accum_out=ssq[:, tt:tt + 1]).then_inc(s["sums_ready"], 1)

            for tt in range(TT):
                act.wait_ge(x_loaded[tt], 16)
                sums(tt, junk)
            act.wait_ge(s["gain_ones"], 1)
            for dst, name in ((gq66[0:HD], "g_fox_q"), (gk66[0:HD], "g_fox_k"), (gq2[0:HD], "g_diff_q"),
                              (gq2[HD:P], "g_diff_q"), (gk2[0:HD], "g_diff_k"), (gk2[HD:P], "g_diff_k"),
                              (gsub, "g_subln")):
                act.dma_start(dst, a[name].rearrange("a p -> p a")).then_inc(s["head_loaded"], 16)
            for i, name in enumerate(("lambda_q1", "lambda_k1", "lambda_q2", "lambda_k2")):
                act.dma_start(lamv[:, i, :], bass.AP(a[name].tensor, a[name].offset,
                                                     [[0, P], [1, HD]])).then_inc(s["head_loaded"], 16)
            act.dma_start(wr[:, :, :], rows(a["w_router"][0])).then_inc(s["router_loaded"], 16)
            act.wait_ge(s["vrow_T"], 1)
            c.copy(vrow[0:DIFF_HEADS, :], B[7][0:DIFF_HEADS, 0:VROW]).then_inc(s["vrow_ready"], 1)

            act.wait_ge(s["z_ready"], 1)
            tn.link(c.activation(ze, zn, ACT.Exp))
            act.wait_ge(s["lam_ready"], 1)
            c.activation(lam[:, 2:4], lam[:, 0:2], ACT.Exp).then_inc(s["lam_exp"], 1)
            c.activation(ze, ze, ACT.Ln, bias=one).then_inc(s["fe_ready"], 1)

            def tr_copy(j, dst, src, scale):
                act.wait_ge(s["turned"], j + 1)
                c.activation(dst, src, ACT.Copy if isinstance(scale, float) else ACT.Identity,
                             scale=scale).then_inc(s["turned_copied"], 1)

            act.wait_ge(s["gain_scaled"], 1)
            j = 0
            for step, i in ORDER:
                if step == "proj":
                    act.wait_ge(s["proj_done"], i + 1)
                    if i in QK_UNITS:
                        act.wait_ge(s["mean_ready"], powers_before[step, i])
                        c.activation(sq, B[i % 2][:, :], ACT.Square).then_inc(s["sq_ready"], 1)
                    else:
                        c.copy((fv if i < 6 else dv)[:, i % 2, :], B[i % 2][:, :]).then_inc(s["v_copied"], 1)
                elif step == "qkT":
                    tt = i % 2
                    if i < 4:
                        dst, gain = (fqT, gq66) if i < 2 else (fkT, gk66)
                        for b in range(2):
                            tr_copy(j, dst[0:AUG, 4 * b:4 * b + 4, tt * P:(tt + 1) * P],
                                    TRB[j % 2][0:AUG, :].rearrange("p (h t) -> p h t", h=4), gain[0:AUG])
                            j += 1
                    else:
                        dst, gain = (dqT, gq2) if i < 8 else (dkT, gk2)
                        tr_copy(j, dst[:, :, tt * P:(tt + 1) * P],
                                TRB[j % 2][:, :].rearrange("p (h t) -> p h t", h=4), gain)
                        j += 1
                elif step == "sc":
                    act.wait_ge(s["sc_max"], i + 1)
                    w, n = S[buf(i)], buf(i)
                    c.activation(w[:, 0:P], w[:, 0:P], ACT.Exp, bias=nmax[:, n, 0:1],
                                 accum_out=esum[:, n, 0:1]).then_inc(s["exp_done"], 1)
                    c.activation(w[:, P:VROW], w[:, P:VROW], ACT.Exp, bias=nmax[:, n, 1:2],
                                 accum_out=esum[:, n, 1:2]).then_inc(s["exp_done"], 1)
                elif step == "pt":
                    if i >= 2:
                        act.wait_ge(s["pv_done"], i - 1)
                    tr_copy(j, PT[i % 2], TRB[j % 2][:, 0:VROW], 1.0)
                    j += 1
                elif step == "pv" and i >= 8:
                    act.wait_ge(s["pv_done"], i + 1)
                    act.wait_ge(s["pow_done"], powers_before[step, i])
                    for b in range(TT):
                        ins = c.activation(sq[:, b * DV:(b + 1) * DV], B[6 + i % 2][:, b * DV:(b + 1) * DV],
                                           ACT.Square, scale=rsum[:, first_sum(i), b:b + 1], accum_out=dms[:, b:b + 1])
                        ins.then_inc(s["dsum_ready"], 1)
                elif step == "mix":
                    for tt in range(TT):
                        tr_copy(j, aT[:, 4 * i:4 * i + 4, tt * P:(tt + 1) * P],
                                TRB[j % 2][:, :].rearrange("p (h t) -> p h t", h=4), gsub if i else 1.0)
                        j += 1
            act.dma_start(bcol[0:E, :], a["b_router"].rearrange("a p -> p a")).then_inc(s["router_loaded"], 16)

            def half_sums(ready, scratch):
                for tt in range(TT):
                    for half, dst in enumerate((halfsum, ssq)):
                        act.wait_ge(s[ready], 2 * tt + half + 1)
                        cols = slice(half * 512, (half + 1) * 512)
                        c.activation(scratch[:, tt, cols], hres[:, tt, cols], ACT.Square,
                                     accum_out=dst[:, tt:tt + 1]).then_inc(s["sums_ready"], 1)

            half_sums("res_ready", mid_junk)
            for tt in range(TT):
                act.wait_ge(s["top_ready"], tt + 1)
                c.activation(e4[:, tt, :], mx8[:, tt, 0:TOPK], ACT.Exp, bias=nv0[:, tt:tt + 1],
                             accum_out=es[:, tt:tt + 1]).then_inc(s["gate_exp"], 1)

            act.wait_ge(s["tables_ready"], 1)
            n = act.value_load(ints[0:1, EXTRA:EXTRA + 1], min_val=0, max_val=EXTRA)
            with act.Fori(0, (n + 1) // 2 + E // 2) as p:
                for i in range(2):
                    act.wait_ge(s["glu_ready"], 2 * p + (i + 1))
                    c.activation(sig, glu, ACT.Sigmoid, scale=ALPHA).then_inc(s["sig_ready"], 1)
                    if i == 0:
                        act.wait_ge(s["sgt_done"], p + 1)
                        c.copy(SGT.rearrange("p a t -> p (a t)"), GB[:, :]).then_inc(s["sgt_taken"], 1)
                    act.wait_ge(s["hT_done"], 2 * p + (i + 1))
                    c.copy(hT.rearrange("p k c -> p (k c)"), TB[:, :]).then_inc(s["hT_taken"], 1)
                    act.wait_ge(s["chunk_used"], 2 * RING * p + (i + 1) * RING)
                    c.copy(outs[0:SLOTS, i, :], TB[0:SLOTS, :])
                    c.copy(outs[SLOTS:P, 1 - i, :], TB[SLOTS:P, :]).then_inc(s["out_taken"], 1)

            half_sums("y_taken", ring[:, 5:7, 0:D])
            for q, (tt, c0, n) in enumerate(PARTS):
                act.wait_ge(s["gate_done"], q + 1)
                c.activation(ring[:, q, 0:n], gate_bank(tt, c0, n), ACT.Sigmoid).then_inc(s["sigmoid_ready"], 1)

        @block.tensor
        def _(pe):
            mm, tr = nc.tensor.matmul, nc.tensor.transpose
            pe.wait_ge(s["consts_made"], 2)
            pe.wait_ge(s["vec_loaded"], 16 * 5)
            tr(B[0][:, 0:3 * KD], grow[0:3 * KD, :], ident[0:3 * KD, 0:3 * KD]).then_inc(s["gcols_T"], 1)
            pe.wait_ge(s["masked_bucket"], 1)
            mm(B[7][0:DIFF_HEADS, 0:VROW], relb[0:BUCKETS + 1, :], bucket[0:BUCKETS + 1, :],
               start=True, stop=True).then_inc(s["vrow_T"], 1)

            def turn_x(k, tt, banks):
                pe.wait_ge(s["xn_ready"], TT * k + tt + 1)
                for b in range(2):
                    for m in range(4):
                        ins = tr(banks[2 * tt + b][:, m * P:(m + 1) * P],
                                 xn[:, tt, (4 * b + m) * P:(4 * b + m + 1) * P], ident[:, :])
                    ins.then_inc(s["xT_done"], 1)

            for tt in range(TT):
                turn_x(0, tt, B[2:6])
            pe.wait_ge(s["wf_loaded"], 32)
            for tt in range(TT):
                pe.wait_ge(s["xT_ready"], 2 * tt + 2)
                for k in range(KD):
                    ins = mm(B[6][0:8, tt * P:(tt + 1) * P], wf[:, k, :], aT[:, k, tt * P:(tt + 1) * P],
                             start=(k == 0), stop=(k == KD - 1))
            ins.then_inc(s["fT_done"], 1)
            pe.wait_ge(s["fT_copied"], 1)
            for tt in range(TT):
                ins = tr(B[6][:, T + 8 * tt:T + 8 * tt + 8], fT[0:8, tt * P:(tt + 1) * P], ident[0:8, 0:8])
            ins.then_inc(s["f_done"], 1)

            j = 0

            def bank_turn():
                if j >= 2:
                    pe.wait_ge(s["turned_copied"], j - 1)
                return TRB[j % 2]

            def project(q, part):
                tt, half = q // 2, q % 2
                for k in range(4 * part, 4 * part + 4):
                    ins = mm(B[q][:, :], aT[:, k, tt * P:(tt + 1) * P], wide[:, k, half * 512:(half + 1) * 512],
                             start=(k == 0), stop=(k == KD - 1))
                if part:
                    ins.then_inc(s["out_done"], 1)

            for step, i in ORDER:
                if step == "proj":
                    g, tt = i // 2, i % 2
                    if i == 0:
                        pe.wait_ge(s["gcols_ready"], 1)
                    if i >= 2:
                        unit_free(pe, i - 2)
                    for k in range(KD):
                        if k % 4 == 0:
                            pe.wait_ge(win_loaded[2 * g + k // 4], 16)
                        ins = mm(B[i % 2][:, :], aT[:, k, tt * P:(tt + 1) * P],
                                 ring[:, 2 * g + k // 4, (k % 4) * GROUP:(k % 4 + 1) * GROUP],
                                 start=(k == 0), stop=(k == KD - 1))
                    ins.then_inc(s["proj_done"], 1)
                elif step == "cum":
                    pe.wait_ge(s["logf_ready"], 1)
                    pe.wait_ge(s["vrow_ready"], 1)
                    mm(B[7][:, 0:8], upper[:, :], logf[:, 0, :], start=True, stop=True)
                    mm(B[7][:, 8:16], ones[:, :], logf[:, 0, :], start=True, stop=False)
                    mm(B[7][:, 8:16], upper[:, :], logf[:, 1, :], start=False, stop=True).then_inc(s["cum_done"], 1)
                elif step == "qkT":
                    pe.wait_ge(s["qk_ready" if i < 4 else "qk_scaled"], QK_UNITS.index(i) + 1)
                    if i < 4:
                        for b in range(2):
                            bank = bank_turn()
                            for h in range(4):
                                ins = tr(bank[0:AUG, h * P:(h + 1) * P], qkn[i % 2][:, 4 * b + h, :], ident[:, :])
                            ins.then_inc(s["turned"], 1)
                            j += 1
                    else:
                        bank = bank_turn()
                        for h in range(4):
                            ins = tr(bank[:, h * P:(h + 1) * P], qkn_flat[i % 2][:, h * P:(h + 1) * P], ident[:, :])
                        ins.then_inc(s["turned"], 1)
                        j += 1
                elif step == "sc":
                    bank = B[2 + i % 2]
                    if i == 0:
                        pe.wait_ge(s["turned_copied"], 8)
                    if i == 8:
                        pe.wait_ge(s["turned_copied"], turned_after["qkT", 9])
                    if i >= 2:
                        pe.wait_ge(s["sc_masked"], i - 1)
                    if i < 8:
                        q, k = fqT[0:AUG, i, :], fkT[0:AUG, i, :]
                    else:
                        h, m = (i - 8) // 2, i % 2
                        q, k = dqT[m * HD:(m + 1) * HD, h, :], dkT[m * HD:(m + 1) * HD, h, :]
                    mm(bank[:, 0:P], q[:, 0:P], k[:, 0:P], start=True, stop=True)
                    mm(bank[:, P:VROW], q[:, P:T], k[:, :], start=True, stop=True).then_inc(s["sc_done"], 1)
                elif step == "pt":
                    if i < 8:
                        pe.wait_ge(s["exp_done"], 2 * i + 2)
                    else:
                        pe.wait_ge(s["comb_ready"], i - 7)
                    bank, w = bank_turn(), S[first_buf(i)]
                    for b in range(3):
                        ins = tr(bank[:, b * P:(b + 1) * P], w[:, b * P:(b + 1) * P], ident[:, :])
                    ins.then_inc(s["turned"], 1)
                    j += 1
                elif step == "pv":
                    bank, w = B[6 + i % 2], PT[i % 2]
                    pe.wait_ge(s["turned_copied"], turned_after["pt", i])
                    if i >= 2:
                        pe.wait_ge(s["pv_taken"], i - 1)
                    if i < 8:
                        v, n = [fv[:, t, i * HD:(i + 1) * HD] for t in range(TT)], HD
                    else:
                        v, n = [dv[:, t, (i - 8) * DV:(i - 7) * DV] for t in range(TT)], DV
                    if i in (0, 8):
                        pe.wait_ge(s["v_copied"], 2 if i < 8 else 4)
                    mm(bank[:, 0:n], w[:, 0:P], v[0], start=True, stop=True)
                    mm(bank[:, n:2 * n], w[:, P:T], v[0], start=True, stop=False)
                    mm(bank[:, n:2 * n], w[:, T:VROW], v[1], start=False, stop=True).then_inc(s["pv_done"], 1)
                elif step == "out":
                    if i == 0:
                        pe.wait_ge(s["wout_loaded"], 16)
                        pe.wait_ge(s["turned_copied"], turned_after["mix", 0])
                    if i < 2:
                        unit_free(pe, 10 + i)
                    else:
                        pe.wait_ge(s["sc_masked"], 13 + i)
                    project(i, 0)
                elif step == "mix":
                    pe.wait_ge(s["pv_taken"], 12 if i else 8)
                    for tt in range(TT):
                        bank = bank_turn()
                        for b in range(4):
                            ins = tr(bank[:, b * P:(b + 1) * P], xn[:, tt, (4 * i + b) * P:(4 * i + b + 1) * P],
                                     ident[:, :])
                        ins.then_inc(s["turned"], 1)
                        j += 1
            def router(tt):
                for k in range(KD):
                    if k % 4 == 0:
                        pe.wait_ge(s["xT_ready"], 4 + (2 if tt == 0 else 2 + k // 4 + 1))
                    ins = mm(B[5][0:E, tt * P:(tt + 1) * P], wr[:, k, :], aT[:, k, tt * P:(tt + 1) * P],
                             start=(k == 0), stop=(k == KD - 1))
                ins.then_inc(s["logitsT_done"], 1)

            def turn_logits(tt):
                pe.wait_ge(s["lT_ready"], tt + 1)
                tr(B[5][:, T + tt * E:T + (tt + 1) * E], lT[0:E, tt * P:(tt + 1) * P],
                   ident[0:E, 0:E]).then_inc(s["logits_done"], 1)

            pe.wait_ge(s["turned_copied"], j)
            project(0, 1)
            project(1, 1)
            project(2, 1)
            turn_x(1, 0, B[4:8])
            project(3, 1)
            pe.wait_ge(s["router_loaded"], 32)
            router(0)
            turn_logits(0)
            turn_x(1, 1, B[4:8])
            router(1)
            turn_logits(1)
            pe.wait_ge(s["mask_ready"], 1)
            mm(B[2][:, 0:E], upper[:, :], M[:, 0, :], start=True, stop=True)
            mm(B[2][:, E:2 * E], ones[:, :], M[:, 0, :], start=True, stop=False)
            mm(B[3][0:E, 0:1], M[:, 0, :], ones[:, 0:1], start=True, stop=False)
            pe.wait_ge(s["mask_ready"], 2)
            mm(B[2][:, E:2 * E], upper[:, :], M[:, 1, :], start=False, stop=True)
            mm(B[3][0:E, 0:1], M[:, 1, :], ones[:, 0:1], start=False, stop=True).then_inc(s["ranks_done"], 1)

            def gather(b):
                for k in range(4):
                    for tt in range(TT):
                        ins = mm(GB[:, k * P:(k + 1) * P], xn[:, tt, (4 * b + k) * P:(4 * b + k + 1) * P],
                                 Sel[:, tt, :], start=(k == 0 and tt == 0), stop=(tt == 1), skip_group_check=True)
                ins.then_inc(s["gath_done"], 1)

            def combine(last=False):
                for q in range(4):
                    tt, half = q // 2, q % 2
                    ins = mm(Y[q][:, :], SGT[:, half, tt * P:(tt + 1) * P], outs[:, half, :],
                             start=False, stop=False, skip_group_check=True)
                    if last:
                        ins.then_inc(s["y_done"], 1)

            pe.wait_ge(s["ranks_taken"], 1)
            for q, table in enumerate((P1i, Gi)):
                for tt in range(TT):
                    ins = tr(B[4][0:E, q * T + tt * P:q * T + (tt + 1) * P], table[:, tt, 0:E], ident[:, :])
            ins.then_inc(s["byexpert_T"], 1)
            pe.wait_ge(s["extra_ready"], 1)
            mm(B[5][0:E, 0:1], upper[0:E, 0:E], extra[0:E, :], start=True, stop=True)
            mm(B[5][0:1, 1:2], ones[0:E, 0:1], extra[0:E, :], start=True, stop=True).then_inc(s["offs_done"], 1)
            pe.wait_ge(s["sel_ready"], 1)
            gather(0)
            pe.wait_ge(s["b_loaded"], 32)
            pe.wait_ge(s["byexpert_ready"], 1)
            for q in range(4):
                tt, half = q // 2, q % 2
                ins = mm(Y[q][:, :], GT[:, tt * P:(tt + 1) * P], b2r[:, half * 512:(half + 1) * 512],
                         start=True, stop=False, skip_group_check=True)
            ins.then_inc(s["b_used"], 1)
            pe.wait_ge(s["items_ready"], 1)
            w = EXTRA + 2
            for tt in range(TT):
                mm(TB[:, tt * w:(tt + 1) * w], P1T[0:E, tt * P:(tt + 1) * P], Eall[0:E, E:COLS],
                   start=True, stop=False)
                mm(TB[:, tt * w:(tt + 1) * w], ones[0:E, :], Bneg[0:E, :], start=False, stop=True)
                mm(TB[:, (TT + tt) * w:(TT + tt + 1) * w], GT[0:E, tt * P:(tt + 1) * P], Eall[0:E, E:COLS],
                   start=True, stop=True)
            mm(TB[0:1, 4 * w:4 * w + EXTRA], iotap[0:E, :], Eall[0:E, E:ITEMS], start=True, stop=True) \
                .then_inc(s["tables_done"], 1)
            pe.wait_ge(s["gath_taken"], 1)
            gather(1)
            pe.wait_ge(s["tables_ready"], 1)
            n = pe.value_load(ints[0:1, EXTRA:EXTRA + 1], min_val=0, max_val=EXTRA)
            pairs = (n + 1) // 2 + E // 2
            def pair(p, first=False):
                def chunk(c, i):
                    return early[c] if first and i == 1 and c < EARLY else ring[:, c, :]

                for i in range(2):
                    if i == 0:
                        pe.wait_ge(s["expert_ready"], p + 1)
                    for g in range(2):
                        for u in range(2):
                            c0 = u * D + g * 512
                            mm(H[u * SLOTS:(u + 1) * SLOTS, g * 512:(g + 1) * 512],
                               expert1[:, i * SLOTS:(i + 1) * SLOTS], b1r[:, c0:c0 + 512], start=True, stop=False)
                    for k in range(KD):
                        if i == 0 and k % 4 == 0:
                            pe.wait_ge(s["gath_taken"], 2 * p + (k // 4 + 1))
                        pe.wait_ge(chunk_loaded[k], (2 * p + (i + 1)) * 16)
                        for g in range(2):
                            for u in range(2):
                                c0 = u * D + g * 512
                                ins = mm(H[u * SLOTS:(u + 1) * SLOTS, g * 512:(g + 1) * 512],
                                         xsel[:, k, i * SLOTS:(i + 1) * SLOTS], chunk(k, i)[:, c0:c0 + 512],
                                         start=False, stop=(k == KD - 1))
                        ins.then_inc(s["chunk_used"], 1)
                    if i == 0:
                        pe.wait_ge(s["out_taken"], 2 * p + 2)
                        pe.wait_ge(s["sgt_taken"], p + 1)
                        combine()
                        pe.wait_ge(s["sg_ready"], p + 1)
                        for v in range(2):
                            for tt in range(TT):
                                ins = tr(GB[:, (2 * v + tt) * P:(2 * v + tt + 1) * P],
                                         SG[:, tt, v * SLOTS:v * SLOTS + P], ident[:, :])
                        ins.then_inc(s["sgt_done"], 1)
                    else:
                        pe.wait_ge(s["sel_ready"], p + 2)
                        pe.wait_ge(s["sgt_taken"], p + 2)
                        gather(0)
                    pe.wait_ge(s["hid_ready"], 2 * p + (i + 1))
                    if i:
                        pe.wait_ge(s["out_taken"], 2 * p + 3)
                    for k in range(4):
                        ins = tr(TB[:, k * P:(k + 1) * P], prod[:, k * P:(k + 1) * P], ident[:, :])
                    ins.then_inc(s["hT_done"], 1)
                    if i:
                        pe.wait_ge(s["gath_taken"], 2 * p + 3)
                        gather(1)
                    pe.wait_ge(s["hT_taken"], 2 * p + (i + 1))
                    for k in range(KD):
                        c = KD + k // 2
                        if k % 2 == 0:
                            pe.wait_ge(chunk_loaded[c], (2 * p + (i + 1)) * 16)
                        for u in range(2):
                            c0 = (k % 2) * D + (u ^ i) * 512
                            ins = mm(TB[u * SLOTS:(u + 1) * SLOTS, :],
                                     hT[:, k % 4, (k // 4) * SLOTS:(k // 4 + 1) * SLOTS], chunk(c, i)[:, c0:c0 + 512],
                                     start=(k == 0), stop=(k == KD - 1))
                        if k % 2:
                            ins.then_inc(s["chunk_used"], 1)
            pair(0, first=True)
            with pe.Fori(1, PLE_PAIR + 1) as p:
                pair(p)
            pe.wait_ge(s["tail_loaded"], 32)
            pe.wait_ge(s["gath_taken"], PLE_PAIR * 2 + 4)
            for k in range(2):
                for tt in range(TT):
                    ins = tr(GB[:, k * T + tt * P:k * T + (tt + 1) * P], pin[:, tt, k * P:(k + 1) * P], ident[:, :])
            ins.then_inc(s["pT_done"], 1)
            pe.wait_ge(s["pT_ready"], 1)
            for q in range(4):
                tt, half = q // 2, q % 2
                if q >= 2:
                    pe.wait_ge(s["pp_taken"], q - 1)
                for k in range(2):
                    ins = mm(B[4 + half][:, :], pT[:, k, tt * P:(tt + 1) * P],
                             wp[:, k, half * 512:(half + 1) * 512], start=(k == 0), stop=(k == 1))
                ins.then_inc(s["pp_done"], 1)
            pe.wait_ge(s["pp_taken"], 4)
            with pe.Fori(PLE_PAIR + 1, pairs) as p:
                pair(p)
            pe.wait_ge(s["out_taken"], pairs * 2 + 2)
            pe.wait_ge(s["sgt_taken"], pairs + 1)
            combine(last=True)
            pe.wait_ge(s["gath_taken"], pairs * 2 + 2)
            turn_x(2, 0, Y)
            pe.wait_ge(s["gate_loaded"], 16)
            for q, (tt, c0, n) in enumerate(PARTS):
                if q == 1:
                    turn_x(2, 1, Y)
                for k in range(KD):
                    if k % 4 == 0:
                        pe.wait_ge(s["xT_ready"], 8 + 2 * tt + k // 4 + 1)
                    ins = mm(gate_bank(tt, c0, n), aT[:, k, tt * P:(tt + 1) * P], wide[:, k, c0:c0 + n],
                             start=(k == 0), stop=(k == KD - 1))
                ins.then_inc(s["gate_done"], 1)

        @block.vector
        def _(dve):
            v = nc.vector
            tn = Turns(dve, s["dve_turn"])
            v.memset(gains, 1.0).then_inc(s["gain_ones"], 1)
            v.memset(relb[BUCKETS:BUCKETS + 1, :], NEG).then_inc(s["masked_bucket"], 1)
            n_pow = 0

            def request(ins):
                nonlocal n_pow
                n_pow += 1
                ins.then_inc(s["mean_ready"], 1)

            def mean(dst, src, n):
                request(v.tensor_scalar(dst, src, 1.0 / n, EPS, ALU.mult, ALU.add))

            def norm_mean(k, tt):
                sq_sum = ssq[:, tt:tt + 1]
                if k:
                    before = (2 * k - 1) * TT + 2 * tt
                    dve.wait_ge(s["sums_ready"], before + 1)
                    part = halfsum[:, tt:tt + 1]
                    tn.link(v.tensor_scalar(part, part, 1.0 / D, EPS, ALU.mult, ALU.add))
                    dve.wait_ge(s["sums_ready"], before + 2)
                    request(v.scalar_tensor_tensor(out=sq_sum, in0=sq_sum, scalar=1.0 / D, in1=part,
                                                   op0=ALU.mult, op1=ALU.add))
                else:
                    dve.wait_ge(s["sums_ready"], tt + 1)
                    mean(sq_sum, sq_sum, D)

            def norm_rows(k, tt):
                dve.wait_ge(s["pow_done"], n_pow)
                v.tensor_scalar(xn[:, tt, :], hres[:, tt, :], rstd[:, tt:tt + 1], None,
                                ALU.mult).then_inc(s["xn_ready"], 1)

            def norm_cols(k, tt, banks):
                for b in range(2):
                    dve.wait_ge(s["xT_done"], 4 * k + 2 * tt + b + 1)
                    v.tensor_tensor(aT[:, 4 * b:4 * b + 4, tt * P:(tt + 1) * P],
                                    banks[2 * tt + b][:, :].rearrange("p (k t) -> p k t", k=4),
                                    spread(gcols[:, KD * k + 4 * b:KD * k + 4 * b + 4], 2, P),
                                    ALU.mult).then_inc(s["xT_ready"], 1)

            def head_constants():
                dve.wait_ge(s["head_loaded"], 16 * 11)
                tn.link(v.tensor_tensor(lamp, lamv[:, 0:4:2, :], lamv[:, 1:4:2, :], ALU.mult))
                v.tensor_reduce(lam[:, 0:2], lamp, X, ALU.add).then_inc(s["lam_ready"], 1)
                v.tensor_scalar(gq66[0:HD], gq66[0:HD], HD ** -0.5, None, ALU.mult)
                v.tensor_scalar(gq2, gq2, HD ** -0.5, None, ALU.mult)
                v.tensor_scalar(gsub, gsub, 1.0 - LAM_INIT, None, ALU.mult).then_inc(s["gain_scaled"], 1)

            for tt in range(TT):
                norm_mean(0, tt)
                norm_rows(0, tt)
            dve.wait_ge(s["gcols_T"], 1)
            v.tensor_copy(gcols[:, :], B[0][:, 0:3 * KD]).then_inc(s["gcols_ready"], 1)
            dve.wait_ge(s["gcols_ready"], 1)
            for tt in range(TT):
                norm_cols(0, tt, B[2:6])
            dve.wait_ge(s["fT_done"], 1)
            v.tensor_copy(fT[0:8, :], B[6][0:8, 0:T]).then_inc(s["fT_copied"], 1)
            dve.wait_ge(s["f_done"], 1)
            dve.wait_ge(s["wf_loaded"], 32)
            tn.link(v.tensor_tensor(z, B[6][:, T:T + 16].rearrange("p (t h) -> p t h", t=TT), spread(bf, 1, TT),
                                    ALU.add))
            tn.link(v.tensor_scalar(zn, z, -1.0, None, ALU.mult))
            v.tensor_tensor(zn, z, zn, ALU.min).then_inc(s["z_ready"], 1)
            tn.link(v.tensor_scalar(zlow, z, 0.0, None, ALU.min))
            head_constants()
            dve.wait_ge(s["lam_exp"], 1)
            tn.link(v.tensor_tensor(lam[:, 4:5], lam[:, 3:4], lam[:, 2:3], ALU.subtract))
            tn.link(v.tensor_scalar(lam[:, 5:6], lam[:, 4:5], -LAM_INIT, None, ALU.add))
            dve.wait_ge(s["fe_ready"], 1)
            v.tensor_tensor(logf, zlow, ze, ALU.subtract).then_inc(s["logf_ready"], 1)

            def beside(i):
                w, tt = qkn[i % 2], i % 2
                gate, plain = (HD, HD + 1) if i < 2 else (HD + 1, HD)
                v.tensor_copy(w[:, :, gate], (cpos if i < 2 else cneg)[:, tt, :])
                v.memset(w[:, :, plain], 1.0).then_inc(s["qk_ready"], 1)

            for step, i in ORDER:
                if step == "cum":
                    dve.wait_ge(s["cum_done"], 1)
                    c = B[7][:, 0:16].rearrange("p (t h) -> p t h", t=TT)
                    v.tensor_copy(cpos, c)
                    tn.link(v.tensor_scalar(cneg, c, -1.0, None, ALU.mult))
                    beside(0)
                elif step == "proj" and i in QK_UNITS:
                    u = QK_UNITS.index(i)
                    dve.wait_ge(s["sq_ready"], u + 1)
                    tn.link(v.tensor_reduce(ms, sq.rearrange("p (h d) -> p h d", h=8), X, ALU.add))
                    mean(ms, ms, HD)
                    dve.wait_ge(s["pow_done"], n_pow)
                    if i in (2, 3, 6, 7, 8, 9):
                        dve.wait_ge(s["turned"], turned_after["qkT", QK_UNITS[u - 2]])
                    dst = qkn[i % 2][:, :, 0:HD] if i < 4 else qkn_flat[i % 2].rearrange("p (h d) -> p h d", h=8)
                    v.tensor_tensor(dst, B[i % 2][:, :].rearrange("p (h d) -> p h d", h=8), spread(qr, 2, HD),
                                    ALU.mult).then_inc(s["qk_scaled"], 1)
                    if 0 < i < 4:
                        beside(i)
                elif step == "sc":
                    w, bank, m = S[buf(i)], B[2 + i % 2], buf(i)
                    dve.wait_ge(s["sc_done"], i + 1)
                    if 2 <= i < 10:
                        dve.wait_ge(s["turned"], turned_after["pt", i - 2])
                    elif i >= 12:
                        dve.wait_ge(s["turned"], turned_after["pt", i // 2 + 2])
                    elif i >= 10:
                        dve.wait_ge(s["turned"], turned_after["qkT", 9])
                    if i == 0:
                        dve.wait_ge(s["consts_made"], 3)
                        dve.wait_ge(s["skew_stored"], 16)
                    if i == 8:
                        dve.wait_ge(s["t5_loaded"], 16)
                    bias = fmask if i < 8 else t5[:, (i - 8) // 2, :]
                    v.tensor_tensor(w[:, 0:P], bank[:, 0:P], bias[:, P:T], ALU.add)
                    v.tensor_tensor(w[:, P:VROW], bank[:, P:VROW], bias, ALU.add).then_inc(s["sc_masked"], 1)
                    dve.wait_ge(s["sc_masked"], i + 1)
                    v.tensor_reduce(nmax[:, m, 0:1], w[:, 0:P], X, ALU.max, negate=True)
                    v.tensor_reduce(nmax[:, m, 1:2], w[:, P:VROW], X, ALU.max,
                                    negate=True).then_inc(s["sc_max"], 1)
                elif step == "pt" and i < 8:
                    dve.wait_ge(s["exp_done"], 2 * i + 2)
                    tn.link(v.reciprocal(rsum[:, i % 2, :], esum[:, i % 2, :]))
                elif step == "pt":
                    dve.wait_ge(s["exp_done"], 4 * (i - 8) + 20)
                    n = first_buf(i)
                    first, second = S[n], S[n + 1]
                    m = first_sum(i)
                    tn.link(v.reciprocal(rsum[:, m:m + 2, :], esum[:, n:n + 2, :]))
                    tn.link(v.scalar_tensor_tensor(out=nl, in0=rsum[:, m + 1, :], scalar=lam[:, 5:6],
                                                   in1=esum[:, n, :], op0=ALU.mult, op1=ALU.mult))
                    v.scalar_tensor_tensor(out=first[:, 0:P], in0=second[:, 0:P], scalar=nl[:, 0:1],
                                           in1=first[:, 0:P], op0=ALU.mult, op1=ALU.add)
                    v.scalar_tensor_tensor(out=first[:, P:VROW], in0=second[:, P:VROW], scalar=nl[:, 1:2],
                                           in1=first[:, P:VROW], op0=ALU.mult,
                                           op1=ALU.add).then_inc(s["comb_ready"], 1)
                    dve.wait_ge(s["comb_ready"], i - 7)
                elif step == "pv":
                    bank, n = B[6 + i % 2], HD if i < 8 else DV
                    if i < 8:
                        dve.wait_ge(s["pv_done"], i + 1)
                        r, c0 = rsum[:, i % 2, :], i * HD
                    else:
                        dve.wait_ge(s["dsum_ready"], 2 * (i - 8) + 2)
                        mean(dms, dms, DV)
                        dve.wait_ge(s["pow_done"], n_pow)
                        tn.link(v.tensor_tensor(dr2, dr, rsum[:, first_sum(i), :], ALU.mult))
                        r, c0 = dr2, 512 + (i - 8) * DV
                    v.tensor_tensor(xn[:, :, c0:c0 + n], bank[:, 0:2 * n].rearrange("p (t d) -> p t d", t=TT),
                                    spread(r, 2, n), ALU.mult).then_inc(s["pv_taken"], 1)
                    dve.wait_ge(s["pv_taken"], i + 1)

            def residual(q):
                tt, half = q // 2, q % 2
                dve.wait_ge(s["out_done"], q + 1)
                h = hres[:, tt, half * 512:(half + 1) * 512]
                v.tensor_tensor(h, B[q][:, :], h, ALU.add).then_inc(s["res_ready"], 1)

            def logits_bias(tt):
                dve.wait_ge(s["logitsT_done"], tt + 1)
                dve.wait_ge(s["router_loaded"], 32)
                v.tensor_scalar(lT[0:E, tt * P:(tt + 1) * P], B[5][0:E, tt * P:(tt + 1) * P], bcol[0:E, 0:1], None,
                                ALU.add).then_inc(s["lT_ready"], 1)

            def top(tt):
                lgt, m8 = lg[:, tt, :], mx8[:, tt, :]
                dve.wait_ge(s["logits_done"], tt + 1)
                tn.link(v.tensor_copy(lgt, B[5][:, T + tt * E:T + (tt + 1) * E]))
                tn.link(v.max(m8, lgt))
                v.tensor_scalar(nv0[:, tt:tt + 1], m8[:, 0:1], -1.0, None, ALU.mult).then_inc(s["top_ready"], 1)
                tn.link(v.max_index(idx8[:, tt, :], m8, lgt))
                tn.link(v.tensor_copy(idxf[:, tt, :], idx8[:, tt, :]))
                o4 = oh[:, tt]
                tn.link(v.tensor_tensor(o4, spread(iotae, 1, TOPK), spread(idxf[:, tt, 0:TOPK], 2, E),
                                        ALU.is_equal))
                v.tensor_reduce(M[:, tt, :], o4.rearrange("p j e -> p e j"), X, ALU.add).then_inc(s["mask_ready"], 1)

            def gates(tt):
                dve.wait_ge(s["gate_exp"], tt + 1)
                tn.link(v.reciprocal(es[:, tt:tt + 1], es[:, tt:tt + 1]))
                tn.link(v.tensor_scalar(e4[:, tt, :], e4[:, tt, :], es[:, tt:tt + 1], None, ALU.mult))
                tn.link(v.tensor_tensor(ohg[:, tt], oh[:, tt], spread(e4[:, tt, :], 2, E), ALU.mult))
                v.tensor_reduce(Gi[:, tt, 0:E], ohg[:, tt].rearrange("p j e -> p e j"), X, ALU.add)

            residual(0)
            residual(1)
            norm_mean(1, 0)
            norm_rows(1, 0)
            residual(2)
            norm_cols(1, 0, B[4:8])
            residual(3)
            norm_mean(1, 1)
            logits_bias(0)
            norm_rows(1, 1)
            dve.wait_ge(s["iotas_made"], 4)
            top(0)
            norm_cols(1, 1, B[4:8])
            gates(0)
            v.memset(Eall, 0.0)
            tn.link(v.memset(Bneg[0:E], 0.0))
            v.tensor_copy(Eall[0:E, 0:E], ident[0:E, 0:E])
            logits_bias(1)
            top(1)
            gates(1)
            dve.wait_ge(s["ranks_done"], 1)
            dve.wait_ge(s["mask_ready"], 2)
            v.tensor_tensor(P1i[:, :, 0:E], B[2][:, 0:TT * E].rearrange("p (t e) -> p t e", t=TT), M,
                            ALU.mult).then_inc(s["ranks_taken"], 1)

            def of_pair(table, i):
                cols = table[:, :, bass.ds(i, 2)]
                return spread(cols, 3, SLOTS)

            def four(t, n):
                return t[:, :, 0:n * SLOTS].rearrange("p t (i c) -> p t i c", i=n)

            def select(i):
                v.tensor_tensor(four(Sel, 2), spread(spread(iota1, 1, 2), 1, TT), of_pair(P1i, i),
                                ALU.is_equal).then_inc(s["sel_ready"], 1)

            def weigh(i):
                v.tensor_tensor(four(SG, 2), four(Sel, 2), of_pair(Gi, i), ALU.mult)
                v.tensor_tensor(SG[:, :, 2 * SLOTS:], Sel[:, :, 0:SLOTS],
                                spread(Gi[:, :, bass.ds(i, 1)][:, :, 0], 2, SLOTS), ALU.mult).then_inc(s["sg_ready"], 1)

            def bias_of(i):
                v.tensor_copy(expert1.rearrange("p (i c) -> p i c", i=2),
                              spread(Eall[:, bass.ds(i, 2)], 2, SLOTS)).then_inc(s["expert_ready"], 1)

            def take_tokens(b):
                v.tensor_tensor(xsel[:, 4 * b:4 * b + 4, :], GB[:, :].rearrange("p (k c) -> p k c", k=4),
                                spread(gcols[:, KD + 4 * b:KD + 4 * b + 4], 2, P),
                                ALU.mult).then_inc(s["gath_taken"], 1)

            tn.link(v.tensor_copy(cnt[0:E], B[3][0:E, 0:1]))
            for r in range(MORE):
                ins = v.tensor_scalar(over[0:E, r:r + 1], cnt[0:E], float(SLOTS * (r + 1)), None, ALU.is_gt)
            tn.link(ins)
            v.tensor_reduce(extra[0:E], over[0:E], X, ALU.add).then_inc(s["extra_ready"], 1)
            dve.wait_ge(s["ranks_taken"], 1)
            select(0)
            dve.wait_ge(s["byexpert_T"], 1)
            dve.wait_ge(s["gt_cleared"], 1)
            v.tensor_copy(arena[0:E, 0:2 * T], B[4][0:E, :]).then_inc(s["byexpert_ready"], 1)
            dve.wait_ge(s["sel_ready"], 1)
            dve.wait_ge(s["extra_ready"], 1)
            dve.wait_ge(s["offs_done"], 1)
            v.tensor_copy(ints[0:1, EXTRA:EXTRA + 1], B[5][0:1, 1:2])
            tn.link(v.tensor_tensor(offs[0:E, 0:1], B[5][0:E, 0:1], extra[0:E], ALU.subtract))
            for r in range(1, MORE):
                ins = v.tensor_scalar(offs[0:E, r:r + 1], offs[0:E, 0:1], float(r), None, ALU.add)
            tn.link(ins)
            for r in range(MORE):
                ins = v.tensor_scalar(Er[0:E, r, :], iota16[0:E], offs[0:E, r:r + 1], over[0:E, r:r + 1],
                                      ALU.is_equal, ALU.mult)
            tn.link(ins)
            tail, base = Eall[0:E, E:ITEMS], Bneg[0:E, 0:EXTRA]
            for r in range(MORE):
                v.tensor_tensor(tail, tail, Er[0:E, r, :], ALU.add)
                ins = v.scalar_tensor_tensor(out=base, in0=Er[0:E, r, :], scalar=-float(SLOTS * (r + 1)), in1=base,
                                             op0=ALU.mult, op1=ALU.add)
                if r < MORE - 1:
                    tn.link(ins)
            ins.then_inc(s["items_ready"], 1)
            weigh(0)
            bias_of(0)
            dve.wait_ge(s["gath_done"], 1)
            take_tokens(0)
            dve.wait_ge(s["tables_done"], 1)
            w = EXTRA + 2
            v.tensor_copy(P1i[:, :, E:COLS], TB[:, 0:TT * w].rearrange("p (t i) -> p t i", t=TT))
            v.tensor_copy(Gi[:, :, E:COLS], TB[:, TT * w:2 * TT * w].rearrange("p (t i) -> p t i", t=TT))
            v.tensor_copy(ints[0:1, 0:EXTRA], TB[0:1, 4 * w:4 * w + EXTRA]).then_inc(s["tables_ready"], 1)
            dve.wait_ge(s["gath_done"], 2)
            take_tokens(1)
            dve.wait_ge(s["tables_ready"], 1)
            n = dve.value_load(ints[0:1, EXTRA:EXTRA + 1], min_val=0, max_val=EXTRA)
            pairs = (n + 1) // 2 + E // 2
            before, per = tn.n, 4

            def pair(p):
                tn.base, tn.n = p * per + before, 0
                for i in range(2):
                    dve.wait_ge(s["chunk_used"], 2 * RING * p + (i * RING + KD))
                    v.tensor_scalar(glu, H[:, 0:1024:2], LIMIT, None, ALU.min).then_inc(s["glu_ready"], 1)
                    tn.link(v.tensor_scalar(lin, H[:, 1:1024:2], -LIMIT, LIMIT, ALU.max, ALU.min))
                    tn.link(v.scalar_tensor_tensor(out=lin, in0=lin, scalar=1.0, in1=glu, op0=ALU.add,
                                                   op1=ALU.mult))
                    dve.wait_ge(s["sig_ready"], 2 * p + (i + 1))
                    v.tensor_tensor(prod, lin, sig, ALU.mult).then_inc(s["hid_ready"], 1)
                    if i == 0:
                        select(2 * p + 2)
                        dve.wait_ge(s["sel_ready"], p + 2)
                        dve.wait_ge(s["sgt_done"], p + 1)
                        weigh(2 * p + 2)
                    else:
                        bias_of(2 * p + 2)
                        for b in range(2):
                            dve.wait_ge(s["gath_done"], 2 * p + (b + 3))
                            take_tokens(b)
                assert tn.n == per

            with dve.Fori(0, PLE_PAIR + 1) as p:
                pair(p)
            dve.wait_ge(s["pT_done"], 1)
            v.tensor_copy(pT, GB[:, :].rearrange("p (k t) -> p k t", k=2)).then_inc(s["pT_ready"], 1)
            aside = junk[:, 0, :]
            for q in range(4):
                tt, half = q // 2, q % 2
                dst = wp[:, 1, :] if tt else aside
                dve.wait_ge(s["pp_done"], 4 if tt else q + 1)
                v.tensor_copy(dst[:, half * 512:(half + 1) * 512], B[4 + half][:, :]).then_inc(s["pp_taken"], 1)
            dve.wait_ge(s["pp_taken"], 2)
            v.tensor_copy(wp[:, 0, :], aside).then_inc(s["ple_ready"], 1)
            with dve.Fori(PLE_PAIR + 1, pairs) as p:
                pair(p)

            def add_experts(q):
                tt, half = q // 2, q % 2
                h = hres[:, tt, half * 512:(half + 1) * 512]
                dve.wait_ge(s["y_done"], q + 1)
                v.tensor_tensor(h, Y[q][:, :], h, ALU.add).then_inc(s["y_taken"], 1)

            for q in range(3):
                add_experts(q)
            norm_mean(2, 0)
            add_experts(3)
            norm_rows(2, 0)
            norm_mean(2, 1)
            norm_rows(2, 1)
            for tt in range(TT):
                norm_cols(2, tt, Y)
            dve.wait_ge(s["ple_ready"], 1)
            for q, (tt, c0, n) in enumerate(PARTS):
                g = ring[:, q, 0:n]
                dve.wait_ge(s["sigmoid_ready"], q + 1)
                v.tensor_tensor(g, wp[:, tt, c0:c0 + n], g, ALU.mult).then_inc(s["gated"], 1)
                dve.wait_ge(s["gated"], q + 1)
                v.tensor_tensor(xn[:, tt, c0:c0 + n], g, hres[:, tt, c0:c0 + n], ALU.add).then_inc(s["y_final"], 1)


INPUTS = ["x", "p", "rel_bias", "g_attn", "w_in", "b_f", "g_fox_q", "g_fox_k", "g_diff_q", "g_diff_k",
          "lambda_q1", "lambda_k1", "lambda_q2", "lambda_k2", "g_subln", "w_out", "g_mlp", "w_router", "b_router",
          "w1", "b1", "w2", "b2", "g_ple", "w_ple_gate", "w_ple_proj"]


def bucket_table():
    table = np.zeros((BUCKETS + 1, VROW), np.float32)
    exact = BUCKETS // 2
    for n in range(VROW):
        rel = 2 * P - 1 - n
        if rel < 0:
            bucket = BUCKETS
        elif rel < exact:
            bucket = rel
        else:
            bucket = min(BUCKETS - 1, exact + int(np.log(rel / exact) / np.log(P / exact) * (BUCKETS - exact) + 1e-9))
        table[bucket, n] = 1.0
    return table


def kernel(**inputs):
    import concourse.bacc as bacc
    from concourse.bass_utils import run_bass_kernel_spmd as run

    nc = bacc.Bacc("TRN2", target_bir_lowering=False, num_devices=1)
    arrays, args = {}, {}
    named = {name: np.asarray(inputs[name]) for name in INPUTS}
    named["buckets"] = bucket_table()
    for name, v in named.items():
        arrays[f"in_{name}"] = v
        args[name] = nc.dram_tensor(f"in_{name}", v.shape, mybir.dt.from_np(v.dtype), kind="ExternalInput").ap()
    out = nc.dram_tensor("out_dram", (1, T, D), F32, kind="ExternalOutput").ap()
    build(nc, args, out)
    return run(nc, [arrays], core_ids=[0]).results[0]["out_dram"]
```
